# Optimizing a Trainium2 kernel written in Bass

```python
import jax, jax.numpy as jnp
from jax import lax
import numpy as np

D_MODEL = 1024
BATCH = 1
SEQ = 512
DEPTH = 2
DEC_BATCH = 1
DEC_SEQ = 32
PAST_LEN = 256

CHUNK = 64
D_MIX = D_MODEL
A_HEADS = 4
A_DV = (D_MIX // 2) // A_HEADS
A_DK = A_DV // 2
A_RANK = 16
A_TAU = 16.0
A_QK = A_HEADS * A_DK
A_VW = A_HEADS * A_DV
B_HEADS = 8
B_HD = (D_MIX // 2) // B_HEADS
B_W = B_HEADS * B_HD
B_LEFT_CHUNKS = 8
B_LEFT = B_LEFT_CHUNKS * CHUNK
REL_CLIP = 128
SPLITS = (A_QK, A_QK, A_VW, A_RANK, A_VW, B_W, B_W, B_W)
N_IN = A_QK + A_QK + A_VW + A_RANK + A_VW + B_W + B_W + B_W
D_FF = 2816
EPS = 1e-6

kernel_name = "hybrid_gla_chunkband_streaming_step"

def rmsnorm(x, g):
    x32 = x.astype(jnp.float32)
    y = x32 * lax.rsqrt(jnp.mean(x32 * x32, axis=-1, keepdims=True) + EPS)
    return (y * g.astype(jnp.float32)).astype(x.dtype)

def swiglu(h, wg, wu, wd):
    return (jax.nn.silu(h @ wg) * (h @ wu)) @ wd

def project(h, w_in, w_alpha, b_alpha):
    B, T, _ = h.shape
    z = h @ w_in
    offs = []
    acc = 0
    for s in SPLITS[:-1]:
        acc += s
        offs.append(acc)
    aq, ak, av, ag, ar, bq, bk, bv = jnp.split(z, offs, axis=-1)
    log_a = jax.nn.log_sigmoid((ag @ w_alpha + b_alpha).astype(jnp.float32)) / A_TAU
    hd = lambda t, n: t.reshape(B, T, n, -1)
    return (hd(aq, A_HEADS), hd(ak, A_HEADS), hd(av, A_HEADS), hd(log_a, A_HEADS), ar,
            hd(bq, B_HEADS), hd(bk, B_HEADS), hd(bv, B_HEADS))

def gla_chunked(q, k, v, log_a, s0):
    B, T, H, DK = q.shape
    DV = v.shape[-1]
    c = min(CHUNK, T)
    n = T // c
    f32 = jnp.float32
    q = q.astype(f32).reshape(B, n, c, H, DK) * (DK ** -0.5)
    k = k.astype(f32).reshape(B, n, c, H, DK)
    vv = v.astype(f32).reshape(B, n, c, H, DV)
    b = jnp.cumsum(log_a.astype(f32).reshape(B, n, c, H, DK), axis=2)
    b_last = b[:, :, -1:]
    q_dec = q * jnp.exp(b)
    scores = jnp.einsum('bnihd,bnjhd->bnhij', q_dec, k * jnp.exp(-b))
    causal = jnp.tril(jnp.ones((c, c), dtype=bool))
    scores = jnp.where(causal, scores, 0.0)
    o_intra = jnp.einsum('bnhij,bnjhv->bnihv', scores, vv)
    u = jnp.einsum('bnjhd,bnjhv->bnhdv', k * jnp.exp(b_last - b), vv)
    decay = jnp.exp(b_last[:, :, 0])

    def step(s, inp):
        d, du = inp
        return d[..., None] * s + du, s

    s_final, s_prev = lax.scan(step, s0.astype(f32),
                               (jnp.moveaxis(decay, 1, 0), jnp.moveaxis(u, 1, 0)))
    s_prev = jnp.moveaxis(s_prev, 0, 1)
    o_inter = jnp.einsum('bnihd,bnhdv->bnihv', q_dec, s_prev)
    o = (o_intra + o_inter).reshape(B, T, H, DV).astype(v.dtype)
    return o, s_final

def rel_bias(table, rel):
    return table[:, jnp.clip(rel, -REL_CLIP, REL_CLIP) + REL_CLIP]

def attend(q, k, v, bias, valid):
    s = jnp.einsum('bihd,bjhd->bhij', q, k).astype(jnp.float32) * (q.shape[-1] ** -0.5)
    s = s + bias[None].astype(jnp.float32)
    if valid is not None:
        s = jnp.where(valid, s, -1e30)
    p = jax.nn.softmax(s, axis=-1).astype(v.dtype)
    return jnp.einsum('bhij,bjhd->bihd', p, v)

def band_attn_prompt(q, k, v, bias_table):
    B, T, H, D = q.shape
    n = T // CHUNK
    KB = B_LEFT + CHUNK
    pad = ((0, 0), (B_LEFT, 0), (0, 0), (0, 0))
    kp = jnp.pad(k, pad)
    vp = jnp.pad(v, pad)
    rel = jnp.arange(CHUNK)[:, None] - jnp.arange(KB)[None, :] + B_LEFT
    bias = rel_bias(bias_table, rel)

    def one_chunk(ci):
        start = ci * CHUNK
        qc = lax.dynamic_slice_in_dim(q, start, CHUNK, axis=1)
        kc = lax.dynamic_slice_in_dim(kp, start, KB, axis=1)
        vc = lax.dynamic_slice_in_dim(vp, start, KB, axis=1)
        valid = (start - B_LEFT + jnp.arange(KB)) >= 0
        return attend(qc, kc, vc, bias, valid[None, :])

    out = lax.map(one_chunk, jnp.arange(n))
    return jnp.moveaxis(out, 0, 1).reshape(B, T, H, D)

def band_attn_sample(q, k, v, ck, cv, bias_table):
    T = q.shape[1]
    W = ck.shape[1]
    kk = jnp.concatenate([ck.astype(k.dtype), k], axis=1)
    vv = jnp.concatenate([cv.astype(v.dtype), v], axis=1)
    rel = jnp.arange(T)[:, None] - jnp.arange(W + T)[None, :] + W
    return attend(q, kk, vv, rel_bias(bias_table, rel), None)

def merge(o_gla, r, gla_norm, o_att, attn_norm, w_out):
    B, T = o_gla.shape[:2]
    g = rmsnorm(o_gla, gla_norm).reshape(B, T, A_VW) * jax.nn.silu(r)
    a = rmsnorm(o_att, attn_norm).reshape(B, T, B_W)
    return jnp.concatenate([g, a], axis=-1) @ w_out

def setup_inputs(seed: int = 0) -> dict:
    key = jax.random.key(seed)
    ks = jax.random.split(key, 24)
    nrm = lambda k, shape, scale: jax.random.normal(k, shape, jnp.float32) * scale
    W = min(B_LEFT, PAST_LEN)
    return {
        "x_prompt": nrm(ks[0], (BATCH, SEQ, D_MODEL), 1.0),
        "x_sample": nrm(ks[1], (DEC_BATCH, DEC_SEQ, D_MODEL), 1.0),
        "state_gla": nrm(ks[2], (DEPTH, DEC_BATCH, A_HEADS, A_DK, A_DV), 1.0),
        "cache_k": nrm(ks[3], (DEPTH, DEC_BATCH, W, B_HEADS, B_HD), 1.0),
        "cache_v": nrm(ks[4], (DEPTH, DEC_BATCH, W, B_HEADS, B_HD), 1.0),
        "norm_ffn1": 1.0 + nrm(ks[5], (DEPTH, D_MODEL), 0.02),
        "w_ffn1_gate": nrm(ks[6], (DEPTH, D_MODEL, D_FF), D_MODEL ** -0.5),
        "w_ffn1_up": nrm(ks[7], (DEPTH, D_MODEL, D_FF), D_MODEL ** -0.5),
        "w_ffn1_down": nrm(ks[8], (DEPTH, D_FF, D_MODEL), D_FF ** -0.5),
        "norm_mix": 1.0 + nrm(ks[9], (DEPTH, D_MODEL), 0.02),
        "w_in": nrm(ks[10], (DEPTH, D_MODEL, N_IN), D_MODEL ** -0.5),
        "w_alpha": nrm(ks[11], (DEPTH, A_RANK, A_QK), A_RANK ** -0.5),
        "b_alpha": nrm(ks[12], (DEPTH, A_QK), 0.1),
        "gla_norm": 1.0 + nrm(ks[13], (DEPTH, A_DV), 0.02),
        "attn_bias": nrm(ks[14], (DEPTH, B_HEADS, 2 * REL_CLIP + 1), 0.5),
        "attn_norm": 1.0 + nrm(ks[15], (DEPTH, B_HD), 0.02),
        "w_out": nrm(ks[16], (DEPTH, D_MIX, D_MODEL), D_MIX ** -0.5),
        "norm_ffn2": 1.0 + nrm(ks[17], (DEPTH, D_MODEL), 0.02),
        "w_ffn2_gate": nrm(ks[18], (DEPTH, D_MODEL, D_FF), D_MODEL ** -0.5),
        "w_ffn2_up": nrm(ks[19], (DEPTH, D_MODEL, D_FF), D_MODEL ** -0.5),
        "w_ffn2_down": nrm(ks[20], (DEPTH, D_FF, D_MODEL), D_FF ** -0.5),
        "final_norm": 1.0 + nrm(ks[21], (D_MODEL,), 0.02),
    }

def reference(x_prompt, x_sample, state_gla, cache_k, cache_v,
              norm_ffn1, w_ffn1_gate, w_ffn1_up, w_ffn1_down,
              norm_mix, w_in, w_alpha, b_alpha, gla_norm, attn_bias, attn_norm, w_out,
              norm_ffn2, w_ffn2_gate, w_ffn2_up, w_ffn2_down, final_norm):
    hp, hs = x_prompt, x_sample
    Bp = hp.shape[0]
    Wp = min(B_LEFT, hp.shape[1])
    gla_p, k_p, v_p, gla_s, k_s, v_s = [], [], [], [], [], []
    for l in range(DEPTH):
        hp = hp + 0.5 * swiglu(rmsnorm(hp, norm_ffn1[l]), w_ffn1_gate[l], w_ffn1_up[l], w_ffn1_down[l])
        hs = hs + 0.5 * swiglu(rmsnorm(hs, norm_ffn1[l]), w_ffn1_gate[l], w_ffn1_up[l], w_ffn1_down[l])

        aq, ak, av, la, ar, bq, bk, bv = project(rmsnorm(hp, norm_mix[l]), w_in[l], w_alpha[l], b_alpha[l])
        s0 = jnp.zeros((Bp, A_HEADS, A_DK, A_DV), jnp.float32)
        og, sp = gla_chunked(aq, ak, av, la, s0)
        oa = band_attn_prompt(bq, bk, bv, attn_bias[l])
        hp = hp + merge(og, ar, gla_norm[l], oa, attn_norm[l], w_out[l])
        gla_p.append(sp)
        k_p.append(bk[:, -Wp:])
        v_p.append(bv[:, -Wp:])

        aq, ak, av, la, ar, bq, bk, bv = project(rmsnorm(hs, norm_mix[l]), w_in[l], w_alpha[l], b_alpha[l])
        og, ss = gla_chunked(aq, ak, av, la, state_gla[l])
        oa = band_attn_sample(bq, bk, bv, cache_k[l], cache_v[l], attn_bias[l])
        hs = hs + merge(og, ar, gla_norm[l], oa, attn_norm[l], w_out[l])
        gla_s.append(ss)
        k_s.append(bk)
        v_s.append(bv)

        hp = hp + 0.5 * swiglu(rmsnorm(hp, norm_ffn2[l]), w_ffn2_gate[l], w_ffn2_up[l], w_ffn2_down[l])
        hs = hs + 0.5 * swiglu(rmsnorm(hs, norm_ffn2[l]), w_ffn2_gate[l], w_ffn2_up[l], w_ffn2_down[l])

    y_prompt = rmsnorm(hp, final_norm)
    y_sample = rmsnorm(hs, final_norm)
    return (y_prompt, y_sample,
            jnp.stack(gla_p), jnp.stack(k_p), jnp.stack(v_p),
            jnp.stack(gla_s), jnp.stack(k_s), jnp.stack(v_s))


_drawn_inputs = setup_inputs


def setup_inputs(seed=0):
    import zlib

    import numpy as np

    out = dict(_drawn_inputs(seed))
    spreads = {}
    factors = {'norm_ffn1': 3.46,
     'gla_norm': 18.368,
     'attn_norm': 11.804,
     'norm_ffn2': 6.444,
     'final_norm': 7.512}
    for name, (base, spread) in spreads.items():
        noise = np.random.default_rng([zlib.crc32(name.encode()), seed]).standard_normal(out[name].shape)
        drawn = base * np.exp(spread * noise) if base else spread * noise
        out[name] = __import__('jax').numpy.asarray(drawn.astype(out[name].dtype))
    for name, factor in factors.items():
        out[name] = (out[name] * factor).astype(out[name].dtype)
    return out
```

```python
from contextlib import ExitStack

import concourse.bass as bass
from concourse import mybir
from concourse.alu_op_type import AluOpType as ALU

f32 = mybir.dt.float32
f32r = mybir.dt.float32r
i32 = mybir.dt.int32
ACT = mybir.ActivationFunctionType
AX = mybir.AxisListType

P = 128
DEPTH = 2
D_MODEL = 1024
D_FF = 2816
SEQ, DEC = 512, 32
T = SEQ + DEC
HALF = T // 2
KT = D_MODEL // P
FT = D_FF // P
FH = FT // 2
CH = 64
A_HEADS, A_DK, A_DV, RANK = 4, 64, 128, 16
B_HEADS, HD = 8, 64
CACHE = 256
NKEY = CACHE + T
REL = 128
BAND = 512
EXT = BAND + P
TAU = 16.0
EPS = 1e-6
NEG = -1e30
TT = [(tt * P, P) for tt in range(SEQ // P)] + [(SEQ, DEC)]
NTT = len(TT)

FFN_UNITS = 2 * (2 * FH + KT)
IN_UNITS = 1 + 8 + 1 + 4 + 12
MIX = FFN_UNITS
ALPHA = MIX + 9
OUT = MIX + IN_UNITS
FFN2 = OUT + KT
UNITS = FFN2 + FFN_UNITS
assert UNITS % 2 == 0


def group_columns(u):
    if u == ALPHA:
        return 2 * P
    for first in (0, FFN2):
        if first <= u < first + FFN_UNITS and (u - first) % (2 * FH + KT) >= 2 * FH:
            return FH * P
    return KT * P


class Signal:

    def __init__(self, sem, events):
        self.sem, self.events, self.said = sem, list(events), []
        self.at = {e: i + 1 for i, e in enumerate(self.events)}
        assert len(self.at) == len(self.events)

    def value(self, layer, event):
        return layer * len(self.events) + self.at[event]

    def of(self, event):
        assert self.events[len(self.said)] == event, (event, self.events[len(self.said)])
        self.said.append(event)
        return self.sem, 1


def encoder_step(nc, xT, bias_rev, gains1, gain_mix, gain2, gains_gla, gains_att, b_alpha,
                 gate_up1, down1, gate_up2, down2, w_in, w_alpha, w_out, state, keysT, values,
                 yT, gla_prompt, gla_sample, new_kT, new_v):
    ctx = ExitStack()
    with ctx:
        def sb(name, shape, dt=f32, scope=ctx):
            return scope.enter_context(nc.sbuf_tensor(name, shape, dt))

        def sem(name):
            return ctx.enter_context(nc.semaphore(name))

        x = sb("x", [P, KT, T])
        zh = sb("zh", [P, KT, T], f32r)
        zl = sb("zl", [P, KT, T], f32r)
        raw = [sb(f"raw{s}", [P, FH * P]) for s in range(2)]
        wh = [sb(f"wh{s}", [P, FH * P], f32r) for s in range(2)]
        wl = [sb(f"wl{s}", [P, FH * P], f32r) for s in range(2)]
        S = sb("S", [P, T])
        sq_acc = sb("sq_acc", [P, T])
        sq_tmp = sb("sq_tmp", [P, T])
        tmp = sb("tmp", [P, 2, T])
        sil = sb("sil", [P, T])
        ones = sb("ones", [P, P])
        ident = sb("ident", [P, P])
        g1 = sb("g1", [P, (DEPTH + 1) * KT])
        gm = sb("gm", [P, DEPTH * KT])
        g2 = sb("g2", [P, DEPTH * KT])
        ggla = sb("ggla", [P, DEPTH])
        gatt = sb("gatt", [P, DEPTH])
        balpha = sb("balpha", [P, DEPTH * 2])
        eps = sb("eps", [P, 1])
        restart = sb("restart", [P, T])
        causal = sb("causal", [P, 2, P])
        ext = tmp[:, :, :].rearrange("p a t -> p (a t)")[0:DEPTH * B_HEADS, 0:EXT]
        agf = sil[0:RANK, :]
        agh = sb("agh", [RANK, T], f32r)
        agl = sb("agl", [RANK, T], f32r)
        ssq = sb("ssq", [P, NTT, A_HEADS + B_HEADS])
        rr = sb("rr", [P, NTT, A_HEADS + B_HEADS])

        with ExitStack() as ffn_scope:
            hh = sb("hh", [P, FH, T], f32r, ffn_scope)
            hl = sb("hl", [P, FH, T], f32r, ffn_scope)
        arT = sb("arT", [P, 4, T])
        oA = sb("oA", [P, NTT, 512])
        bqT = sb("bqT", [P, 4, T])
        bkT = sb("bkT", [P, 4, NKEY])
        vT = sb("vT", [P, 4, T])
        with ExitStack() as gla_scope:
            aqkT = sb("aqkT", [P, 4, T], f32, gla_scope)
            kinv = sb("kinv", [P, 2, T], f32, gla_scope)
            la = sb("la", [P, 2, T], f32, gla_scope)
            eb = sb("eb", [P, 2, T], f32, gla_scope)
            av = sb("av", [P, NTT, 512], f32, gla_scope)
            kend = sb("kend", [P, NTT, 256], f32, gla_scope)
            st = sb("st", [P, 2, SEQ // CH + 1, A_DV], f32, gla_scope)
            st_s = sb("st_s", [P, 2, 2, A_DV], f32, gla_scope)
            atm = sb("atm", [P, 2, 2, 2, P], f32, gla_scope)
        bv = sb("bv", [P, NTT, 512])
        cv = sb("cv", [P, CACHE // P, 512])
        bt = sb("bt", [P, B_HEADS, BAND])
        sc = sb("sc", [P, 2, BAND])
        pr = sb("pr", [P, 2, BAND])
        pt = sb("pt", [P, 2, BAND])
        oB = sb("oB", [P, NTT, 512])
        nmax = sb("nmax", [P, NTT, B_HEADS])
        rsum = sb("rsum", [P, NTT, B_HEADS])
        rinv = sb("rinv", [P, NTT, B_HEADS])
        mixf = tmp[:, :, 0:BAND]

        pu = [ctx.enter_context(nc.psum_tensor(f"pu{s}", [P, 2, 512], f32)) for s in range(2)]
        px = [ctx.enter_context(nc.psum_tensor(f"px{s}", [P, 2, 512], f32)) for s in range(2)]
        skew = nc.dram_tensor("skew", [DEPTH, B_HEADS, P, BAND], f32, kind="Internal").ap()
        ext_dram = nc.dram_tensor("ext_dram", [DEPTH * B_HEADS, EXT], f32, kind="Internal").ap()

        def bank(n):
            return px[(n % 4) // 2][:, n % 2, :]

        def pair(s):
            return pu[s][:, :, 0:HALF]

        def two(row):
            return row.rearrange("p (a b) -> p a b", a=2)

        x_loaded = sem("x_loaded")
        waited = sem("waited")
        vec_loaded = sem("vec_loaded")
        ext_loaded = sem("ext_loaded")
        ext_stored = sem("ext_stored")
        skew_stored = sem("skew_stored")
        const_made = sem("const_made")
        ext_made = sem("ext_made")
        raw_loaded = [sem(f"raw_loaded{s}") for s in range(2)]
        hi_ready = sem("hi_ready")
        lo_ready = sem("lo_ready")
        unit_done = sem("unit_done")
        evacuated = sem("evacuated")
        zh_ready = sem("zh_ready")
        z_ready = sem("z_ready")
        sq_step = sem("sq_step")
        stats_done = sem("stats_done")
        rms_ready = sem("rms_ready")
        S_ready = sem("S_ready")
        silu_ready = sem("silu_ready")
        hid_made = sem("hid_made")
        hid_hi = sem("hid_hi")
        hid_ready = sem("hid_ready")
        mix_loaded = sem("mix_loaded")
        gla_in = sem("gla_in")
        bias_loaded = sem("bias_loaded")
        cv_loaded = sem("cv_loaded")
        outs = sem("outs")
        y_stored = sem("y_stored")
        y_ready = sem("y_ready")
        OUTS = 5 * 16

        items = [(qt, h) for qt in range(NTT) for h in range(B_HEADS)]
        uses = [("AVT", tt) for tt in range(NTT)] + [("KT", tt) for tt in range(NTT)]
        for tt in range(NTT):
            uses += [("AT", tt, 0), ("AT", tt, 1), ("U", tt, 0)] + [("U", tt, 1)] * (tt < NTT - 1)
            uses += [("O", tt, 0), ("O", tt, 1)]
        uses += [("V", tt) for tt in range(NTT)]
        for s in range(len(items) + 1):
            if s < len(items):
                uses.append(("SC", s))
            if s >= 1:
                uses.append(("PT", s - 1))
        for tt in range(NTT):
            uses += [("MA", tt), ("MB", tt)]
        use_no = {u: n for n, u in enumerate(uses)}

        pe_out = Signal(sem("pe_out"), uses)
        act_free = Signal(sem("act_free"), [u for u in uses if u[0] in ("AVT", "O", "V", "PT")])
        dve_free = Signal(sem("dve_free"), [u for u in uses if u[0] in ("KT", "AT", "SC", "MA")])
        state_made = Signal(sem("state_made"), [(tt, c, t) for tt in range(NTT)
                                                for c in range(2 if tt < NTT - 1 else 1) for t in range(2)])
        mix_hi = Signal(sem("mix_hi"), [(k, tt) for tt in range(NTT) for k in "AB"])
        mix_ready = Signal(sem("mix_ready"), [(k, tt) for tt in range(NTT) for k in "AB"])
        av_done = Signal(sem("av_done"), items)
        exp_done = Signal(sem("exp_done"), items)
        max_done = Signal(sem("max_done"), items)
        rinv_made = Signal(sem("rinv_made"), range(NTT))
        ob_ready = Signal(sem("ob_ready"), range(NTT))
        act_gate = Signal(sem("act_gate"), ["ag_hi", "abs", "exp_abs", "softplus", "exp", "expinv", "expend",
                                            "silu_r", "rms_a", "rms_b"])
        dve_gate = Signal(sem("dve_gate"), ["ag_lo", "x1", "min", "logsig", "scan0", "scan1", "end_s", "end0",
                                            "end1", "q", "kinv", "kend"])
        squared = Signal(sem("squared"), [(k, tt) for k in "AB" for tt in range(NTT)])
        summed = Signal(sem("summed"), [(k, tt) for k in "AB" for tt in range(NTT)] + ["rr"])
        normed = Signal(sem("normed"), [(tt, k) for tt in range(NTT) for k in "AB"])
        pool_ready = Signal(sem("pool_ready"), ["states", "scores", "mask_bias"])

        def wait_for(engine, signal, layer, event):
            engine.wait_ge(signal.sem, signal.value(layer, event))

        def stand_alone(engine):
            engine.sem_inc(waited, 1)

        def wait_left(engine, layer, u):
            kind = u[0]
            if kind == "U":
                wait_for(engine, state_made, layer, (u[1], u[2], 1))
            elif kind == "MB":
                wait_for(engine, mix_ready, layer, ("B", u[1]))
            elif kind in ("AVT", "O", "V", "PT"):
                wait_for(engine, act_free, layer, u)
            else:
                wait_for(engine, dve_free, layer, u)

        block = ctx.enter_context(nc.Block())

        @block.sync
        def _(sp):
            sp.dma_start(x[:, :, :], xT.rearrange("(k p) t -> p k t", p=P)).then_inc(x_loaded, 16)
            for buf, src in ((g1, gains1), (gm, gain_mix), (g2, gain2), (ggla, gains_gla),
                             (gatt, gains_att), (balpha, b_alpha)):
                sp.dma_start(buf[:, :], src).then_inc(vec_loaded, 16)

            sp.dma_start(ext[:, EXT - 2 * REL - 1:EXT], bias_rev).then_inc(ext_loaded, 16)

            def load(U, slot, columns, src):
                sp.wait_ge(lo_ready, U + 1)
                rows = RANK if columns == 2 * P else P
                sp.dma_start(raw[slot][0:rows, 0:columns], src).then_inc(raw_loaded[slot], 16)

            def ffn_loads(layer, first, gate_up, down):
                for half in range(2):
                    base = layer * UNITS + first + half * (2 * FH + KT)
                    with sp.Fori(0, FH) as m:
                        for j in range(2):
                            src = sp.snap(layer * (2 * FT) + 2 * m + (half * 2 * FH + j))
                            U = sp.snap(base + 2 * m + j)
                            load(U, j, KT * P, gate_up[src])
                    with sp.Fori(0, KT // 2) as i:
                        for j in range(2):
                            src = sp.snap(layer * (2 * KT) + 2 * i + (half * KT + j))
                            U = sp.snap(base + 2 * i + (2 * FH + j))
                            load(U, j, FH * P, down[src])

            with sp.Fori(0, DEPTH) as layer:
                ffn_loads(layer, 0, gate_up1, down1)
                row = layer * (IN_UNITS - 1)
                load(sp.snap(layer * UNITS + MIX), 0, KT * P, w_in[sp.snap(row)])
                with sp.Fori(0, 4) as i:
                    for j in range(2):
                        src = sp.snap(row + 2 * i + (1 + j))
                        load(sp.snap(layer * UNITS + 2 * i + (MIX + 1 + j)), (1 + j) % 2, KT * P, w_in[src])
                load(sp.snap(layer * UNITS + ALPHA), 1, 2 * P, w_alpha[layer])
                with sp.Fori(0, 8) as i:
                    for j in range(2):
                        src = sp.snap(row + 2 * i + (9 + j))
                        load(sp.snap(layer * UNITS + 2 * i + (ALPHA + 1 + j)), j, KT * P, w_in[src])
                with sp.Fori(0, KT // 2) as i:
                    for j in range(2):
                        src = sp.snap(layer * KT + 2 * i + j)
                        load(sp.snap(layer * UNITS + 2 * i + (OUT + j)), j, KT * P, w_out[src])
                ffn_loads(layer, FFN2, gate_up2, down2)
            for m in range(KT):
                sp.wait_ge(y_ready, m + 1)
                sp.dma_start(yT[m * P:(m + 1) * P, :], x[:, m, :]).then_inc(y_stored, 16)
            sp.wait_ge(y_stored, 16 * KT)
            sp.wait_ge(outs, OUTS * DEPTH)

        @block.gpsimd
        def _(pool):
            pool.memset(ones[:, :], 1.0).then_inc(const_made, 1)
            pool.memset(ident[:, :], 0.0).then_inc(const_made, 1)
            pool.memset(eps[:, :], EPS).then_inc(const_made, 1)
            pool.memset(restart[:, :], 1.0).then_inc(const_made, 1)
            pool.memset(causal[:, :, :], 1.0).then_inc(const_made, 1)
            pool.memset(ssq[:, :, :], 1.0).then_inc(const_made, 1)
            pool.wait_ge(const_made, 6)
            pool.affine_select(out=ident[:, :], in_=ident[:, :], compare_op=ALU.not_equal, fill=1.0,
                               base=0, pattern=[[-1, P]], channel_multiplier=1).then_inc(const_made, 1)
            pool.memset(restart[:, 0:T:CH], 0.0).then_inc(const_made, 1)
            pool.affine_select(out=causal[:, :, :], in_=causal[:, :, :], compare_op=ALU.is_ge, fill=0.0,
                               base=0, pattern=[[0, 2], [1, P]], channel_multiplier=-1).then_inc(const_made, 1)
            pool.wait_ge(const_made, 9)
            pool.memset(causal[0:CH, :, CH:P], 0.0).then_inc(const_made, 1)

            pool.wait_ge(ext_made, 1)
            pool.dma_start(ext_dram, ext[:, :]).then_inc(ext_stored, 16)
            pool.wait_ge(ext_stored, 16)
            for l in range(DEPTH):
                src = bass.AP(ext_dram.tensor, l * B_HEADS * EXT + P - 1, [[EXT, B_HEADS], [-1, P], [1, BAND]])
                pool.dma_start(skew[l], src).then_inc(skew_stored, 16)

            def squares(norm, tile_waits):
                base = norm * (2 * KT - 1)
                tile_waits(0)
                pool.tensor_tensor(sq_acc[:, :], x[:, 0, :], x[:, 0, :], ALU.mult).then_inc(sq_step, 1)
                with pool.Fori(1, KT) as m:
                    tile_waits(m)
                    pool.wait_ge(sq_step, base + 2 * m - 1)
                    pool.tensor_tensor(sq_tmp[:, :], x[:, m, :], x[:, m, :], ALU.mult).then_inc(sq_step, 1)
                    pool.wait_ge(sq_step, base + 2 * m)
                    pool.tensor_tensor(sq_acc[:, :], sq_acc[:, :], sq_tmp[:, :], ALU.add).then_inc(sq_step, 1)

            pool.wait_ge(x_loaded, 16)
            squares(0, lambda m: None)
            with pool.Fori(0, DEPTH) as layer:
                U = layer * UNITS
                squares(3 * layer + 1, lambda m: pool.wait_ge(evacuated, U + m + (FFN_UNITS - KT + 3)))
                stand_alone(pool)
                pool.dma_start(bkT[:, :, 0:CACHE], keysT[layer].rearrange("(j p) t -> p j t", p=P)).then_inc(mix_loaded, 16)
                pool.dma_start(st_s[:, :, 0, :], state[layer].rearrange("t p v -> p t v")).then_inc(gla_in, 16)
                pool.memset(st[:, :, 0, :], 0.0).then_inc(*pool_ready.of("states"))
                pool.memset(atm[:, :, :, :, :], 0.0).then_inc(*pool_ready.of("scores"))
                wait_for(pool, act_free, layer, ("O", NTT - 1, 1))
                wait_for(pool, state_made, layer, (NTT - 1, 0, 1))
                stand_alone(pool)
                pool.dma_start(gla_prompt[layer].rearrange("t p v -> p t v"), st[:, :, SEQ // CH, :]).then_inc(outs, 16)
                pool.dma_start(gla_sample[layer].rearrange("t p v -> p t v"), st_s[:, :, 1, :]).then_inc(outs, 16)
                pool.wait_ge(outs, OUTS * layer + 32)
                stand_alone(pool)
                pool.dma_start(cv[:, :, :], values[layer].rearrange("(c p) d -> p c d", p=P)).then_inc(cv_loaded, 16)
                pool.wait_ge(skew_stored, 16 * DEPTH)
                pool.dma_start(bt[:, :, :], skew[layer].rearrange("h p c -> p h c")).then_inc(bias_loaded, 16)
                pool.wait_ge(bias_loaded, 16 * layer + 16)
                stand_alone(pool)
                pool.memset(bt[0:CH, :, BAND - CH:BAND], NEG).then_inc(*pool_ready.of("mask_bias"))

                def head_squares(k, buf, o, tt):
                    rows = TT[tt][1]
                    if tt >= 1:
                        wait_for(pool, summed, layer, (k, tt - 1))
                    pool.tensor_tensor(mixf[0:rows, buf, :], o[0:rows, tt, :], o[0:rows, tt, :], ALU.mult)\
                        .then_inc(*squared.of((k, tt)))

                for tt in range(NTT):
                    head_squares("A", 0, oA, tt)
                pool.wait_ge(evacuated, U + (OUT + 2))
                stand_alone(pool)
                pool.dma_start(new_kT[layer].rearrange("(j p) t -> p j t", p=P), bkT[:, :, CACHE:NKEY]).then_inc(outs, 16)
                wait_for(pool, act_free, layer, ("V", NTT - 1))
                stand_alone(pool)
                pool.dma_start(new_v[layer, 0:SEQ, :].rearrange("(c p) d -> p c d", p=P),
                               bv[:, 0:NTT - 1, :]).then_inc(outs, 16)
                pool.dma_start(new_v[layer, SEQ:T, :], bv[0:DEC, NTT - 1, :]).then_inc(outs, 16)
                for tt in range(NTT):
                    wait_for(pool, ob_ready, layer, tt)
                    head_squares("B", 1, oB, tt)
                pool.wait_ge(outs, OUTS * layer + OUTS)
                squares(3 * layer + 2, lambda m: pool.wait_ge(evacuated, U + m + (OUT + 3)))
                squares(3 * layer + 3, lambda m: pool.wait_ge(evacuated, U + m + (UNITS - KT + 3)))

        @block.tensor
        def _(pe):
            pe.sem_inc(unit_done, 2)

            def products(U, slot, k_tiles, hi, lo, before_k=None):
                pe.wait_ge(lo_ready, U + 3)
                pe.wait_ge(evacuated, U + 1)
                for k in range(k_tiles):
                    if before_k is not None:
                        before_k(k)
                    for n, (w, z) in enumerate(((wh, hi), (wh, lo), (wl, hi))):
                        for a in range(2):
                            mm = pe.matmul(pu[slot][:, a, 0:HALF], w[slot][:, k * P:(k + 1) * P],
                                           z[:, k, a * HALF:(a + 1) * HALF],
                                           start=(k == 0 and n == 0), stop=(k == k_tiles - 1 and n == 2))
                mm.then_inc(unit_done, 1)

            def stats(norm):
                pe.wait_ge(sq_step, norm * (2 * KT - 1) + (2 * KT - 1))
                for a in range(2):
                    mm = pe.matmul(px[0][:, a, 0:HALF], ones[:, :], sq_acc[:, a * HALF:(a + 1) * HALF],
                                   start=True, stop=True)
                mm.then_inc(stats_done, 1)

            def ffn(layer, first, norm, ffn_no):
                for half in range(2):
                    base = layer * UNITS + first + half * (2 * FH + KT)
                    if half == 0:
                        products(base, 0, KT, zh, zl, lambda k: pe.wait_ge(z_ready, norm * KT + (k + 1)))
                        stats(norm)
                        products(base + 1, 1, KT, zh, zl)
                        start = 1
                    else:
                        start = 0
                    with pe.Fori(start, FH) as m:
                        for j in range(2):
                            products(base + 2 * m + j, j, KT, zh, zl)
                    hid = (layer * 2 + ffn_no) * (2 * FH) + half * FH
                    products(base + 2 * FH, 0, FH, hh, hl, lambda k: pe.wait_ge(hid_ready, hid + (k + 2)))
                    products(base + 2 * FH + 1, 1, FH, hh, hl)
                    with pe.Fori(1, KT // 2) as i:
                        for j in range(2):
                            products(base + 2 * i + (2 * FH + j), j, FH, hh, hl)

            def use(layer, u):
                n = use_no[u]
                if n >= 4:
                    wait_left(pe, layer, uses[n - 4])
                    stand_alone(pe)
                return bank(n)

            def transposes(layer, u, blocks, rows_in, rows_out):
                out = use(layer, u)
                for n, b in enumerate(blocks):
                    mm = pe.transpose(out[0:rows_out, n * rows_in:(n + 1) * rows_in], b, ident[0:rows_in, 0:rows_in])
                mm.then_inc(*pe_out.of(u))

            pe.wait_ge(const_made, 10)
            with pe.Fori(0, DEPTH) as layer:
                ffn(layer, 0, 3 * layer, 0)

                norm = 3 * layer + 1
                products(layer * UNITS + MIX, 0, KT, zh, zl, lambda k: pe.wait_ge(z_ready, norm * KT + (k + 1)))
                stats(norm)
                with pe.Fori(0, 4) as i:
                    for j in range(2):
                        products(layer * UNITS + 2 * i + (MIX + 1 + j), (1 + j) % 2, KT, zh, zl)
                pe.wait_ge(lo_ready, layer * UNITS + (ALPHA + 3))
                pe.wait_ge(evacuated, layer * UNITS + (ALPHA + 1))
                wait_for(pe, dve_gate, layer, "ag_lo")
                for t, dst in ((0, pu[1]), (1, px[0])):
                    for a in range(2):
                        for n, (w, z) in enumerate(((wh, agh), (wh, agl), (wl, agh))):
                            mm = pe.matmul(dst[:, a, 0:HALF], w[1][0:RANK, t * P:(t + 1) * P],
                                           z[:, a * HALF:(a + 1) * HALF], start=(n == 0), stop=(n == 2))
                mm.then_inc(unit_done, 1)
                pe.wait_ge(evacuated, layer * UNITS + (ALPHA + 3))
                for tt, (t0, rows) in enumerate(TT):
                    transposes(layer, ("AVT", tt), [vT[:, j, t0:t0 + rows] for j in range(4)], P, rows)
                with pe.Fori(0, 2) as i:
                    for j in range(2):
                        products(layer * UNITS + 2 * i + (ALPHA + 1 + j), j, KT, zh, zl)

                wait_for(pe, dve_gate, layer, "kend")
                for tt, (t0, rows) in enumerate(TT):
                    transposes(layer, ("KT", tt), [aqkT[:, 2 + t, t0:t0 + rows] for t in range(2)], P, rows)
                wait_for(pe, pool_ready, layer, "states")
                pe.wait_ge(gla_in, 16 * layer + 16)
                for tt, (t0, rows) in enumerate(TT):
                    chunks = 2 if tt < NTT - 1 else 1
                    cl = CH if tt < NTT - 1 else DEC
                    for par in range(2):
                        d = slice(A_DK * par, A_DK * par + A_DK)
                        out = use(layer, ("AT", tt, par))
                        for t in range(2):
                            mm = pe.matmul(out[0:rows, t * P:t * P + rows], kinv[d, t, t0:t0 + rows],
                                           aqkT[d, t, t0:t0 + rows], start=True, stop=True)
                        mm.then_inc(*pe_out.of(("AT", tt, par)))
                    wait_for(pe, act_free, layer, ("AVT", tt))
                    wait_for(pe, dve_free, layer, ("KT", tt))
                    stand_alone(pe)
                    for c in range(chunks):
                        j = slice(c * CH, c * CH + cl)
                        out = use(layer, ("U", tt, c))
                        for h in range(A_HEADS):
                            d = slice(A_DK * (h % 2), A_DK * (h % 2) + A_DK)
                            col = (h // 2) * P
                            mm = pe.matmul(out[d, col:col + A_DV], kend[j, tt, h * A_DK:(h + 1) * A_DK],
                                           av[j, tt, h * A_DV:(h + 1) * A_DV], start=True, stop=True)
                        mm.then_inc(*pe_out.of(("U", tt, c)))
                    if tt < NTT - 1:
                        wait_for(pe, state_made, layer, (tt, 0, 1))
                        stand_alone(pe)
                    for par in range(2):
                        d = slice(A_DK * par, A_DK * par + A_DK)
                        out = use(layer, ("O", tt, par))
                        wait_for(pe, dve_free, layer, ("AT", tt, par))
                        stand_alone(pe)
                        for t in range(2):
                            h = 2 * t + par
                            cols = slice(t * A_DV, (t + 1) * A_DV)
                            pe.matmul(out[0:rows, cols], atm[0:rows, tt % 2, par, t, 0:rows],
                                      av[0:rows, tt, h * A_DV:(h + 1) * A_DV],
                                      start=True, stop=False, skip_group_check=True)
                            for c in range(chunks):
                                before = st[d, t, 2 * tt + c, :] if tt < NTT - 1 else st_s[d, t, 0, :]
                                mm = pe.matmul(out[c * CH:c * CH + cl, cols],
                                               aqkT[d, t, t0 + c * CH:t0 + c * CH + cl], before,
                                               start=False, stop=True, skip_group_check=True)
                        mm.then_inc(*pe_out.of(("O", tt, par)))

                with pe.Fori(2, 8) as i:
                    for j in range(2):
                        products(layer * UNITS + 2 * i + (ALPHA + 1 + j), j, KT, zh, zl)
                pe.wait_ge(evacuated, layer * UNITS + (OUT + 2))
                for tt, (t0, rows) in enumerate(TT):
                    transposes(layer, ("V", tt), [vT[:, j, t0:t0 + rows] for j in range(4)], P, rows)

                pe.wait_ge(mix_loaded, 16 * layer + 16)
                pe.wait_ge(cv_loaded, 16 * layer + 16)
                for s in range(len(items) + 2):
                    if s < len(items):
                        qt, h = items[s]
                        t0, rows = TT[qt]
                        d = slice(HD * (h % 2), HD * (h % 2) + HD)
                        out = use(layer, ("SC", s))
                        q = bqT[d, h // 2, t0:t0 + rows]
                        if qt < NTT - 1:
                            spans = [(0, CACHE, P * (qt + 1))]
                        else:
                            spans = [(0, 0, CACHE), (CACHE, CACHE + SEQ, DEC)]
                        for at, key, n in spans:
                            mm = pe.matmul(out[0:rows, at:at + n], q, bkT[d, h // 2, key:key + n],
                                           start=True, stop=True)
                        mm.then_inc(*pe_out.of(("SC", s)))
                    if 1 <= s <= len(items):
                        n = s - 1
                        qt, h = items[n]
                        rows = TT[qt][1]
                        out = use(layer, ("PT", n))
                        wait_for(pe, exp_done, layer, (qt, h))
                        stand_alone(pe)
                        tiles = [(kt * P, P) for kt in range(qt + 1)] if qt < NTT - 1 else [(0, P), (P, P), (2 * P, DEC)]
                        for kt, (c0, nk) in enumerate(tiles):
                            mm = pe.transpose(out[0:nk, kt * P:kt * P + rows], pr[0:rows, n % 2, c0:c0 + nk],
                                              ident[0:rows, 0:rows])
                        mm.then_inc(*pe_out.of(("PT", n)))
                    if s >= 2:
                        n = s - 2
                        qt, h = items[n]
                        rows = TT[qt][1]
                        if h == 0 and qt == NTT - 1:
                            wait_for(pe, ob_ready, layer, 0)
                        out = pu[(qt % 4) // 2][0:rows, qt % 2, h * HD:(h + 1) * HD]
                        wait_for(pe, act_free, layer, ("PT", n))
                        stand_alone(pe)
                        if qt < NTT - 1:
                            vs = [(P, bv[0:P, kt, h * HD:(h + 1) * HD]) for kt in range(qt + 1)]
                        else:
                            vs = [(P, cv[0:P, kt, h * HD:(h + 1) * HD]) for kt in range(2)]
                            vs += [(DEC, bv[0:DEC, NTT - 1, h * HD:(h + 1) * HD])]
                        for kt, (nk, v) in enumerate(vs):
                            mm = pe.matmul(out, pt[0:nk, n % 2, kt * P:kt * P + rows], v,
                                           start=(kt == 0), stop=(kt == len(vs) - 1))
                        mm.then_inc(*av_done.of((qt, h)))

                for tt, (t0, rows) in enumerate(TT):
                    for i, (k, o) in enumerate((("MA", oA), ("MB", oB))):
                        wait_for(pe, normed, layer, (tt, "AB"[i]))
                        stand_alone(pe)
                        out = use(layer, (k, tt))
                        for j in range(4):
                            mm = pe.transpose(out[:, j * rows:(j + 1) * rows], o[0:rows, tt, j * P:(j + 1) * P],
                                              ident[0:rows, 0:rows])
                        mm.then_inc(*pe_out.of((k, tt)))

                wait_for(pe, mix_ready, layer, ("B", NTT - 1))
                stand_alone(pe)
                with pe.Fori(0, KT // 2) as i:
                    for j in range(2):
                        products(layer * UNITS + 2 * i + (OUT + j), j, KT, zh, zl)

                ffn(layer, FFN2, 3 * layer + 2, 1)
            stats(3 * DEPTH)

        @block.scalar
        def _(act):
            def split_hi(U, slot, columns):
                rows = RANK if columns == 2 * P else P
                act.wait_ge(raw_loaded[slot], (U - slot) * 8 + 16)
                act.wait_ge(unit_done, U + 1)
                act.activation(wh[slot][0:rows, 0:columns], raw[slot][0:rows, 0:columns], ACT.Copy).then_inc(hi_ready, 1)

            def norm_hi(m, gain, wait):
                wait()
                act.activation(zh[:, m, :], x[:, m, :], ACT.Copy, scale=gain).then_inc(zh_ready, 1)

            def rms_of(norm):
                act.wait_ge(stats_done, norm + 1)
                act.activation(two(S[:, :]), px[0][:, :, 0:HALF], ACT.Sqrt, bias=eps[:, :],
                               scale=1.0 / D_MODEL).then_inc(rms_ready, 1)

            def ffn(layer, first, norm, ffn_no):
                for half in range(2):
                    base = layer * UNITS + first + half * (2 * FH + KT)
                    hid = (layer * 2 + ffn_no) * (2 * FH) + half * FH

                    def tile(m, columns):
                        split_hi(base + 2 * m + 2, 0, columns)
                        act.wait_ge(evacuated, base + 2 * m + 3)
                        act.activation(sil[:, :], tmp[:, 0, :], ACT.Silu).then_inc(silu_ready, 1)
                        split_hi(base + 2 * m + 3, 1, columns)
                        act.wait_ge(hid_made, hid + m + 1)
                        act.activation(hh[:, m, :], tmp[:, 1, :], ACT.Copy).then_inc(hid_hi, 1)

                    if half == 0:
                        rms_of(norm)
                    with act.Fori(0, FH - 1) as m:
                        tile(m, KT * P)
                    tile(FH - 1, FH * P)

                    down = base + 2 * FH
                    last = half == 1

                    def unit(m, slot, split):
                        if split:
                            split_hi(down + m + 2, slot, split)
                        if last:
                            gains, at = (gm, layer * KT) if ffn_no == 0 else (g1, (layer + 1) * KT)
                            norm_hi(m, gains[:, bass.ds(at + m, 1)],
                                    lambda: act.wait_ge(evacuated, down + m + 3))

                    with act.Fori(0, KT // 2 - 1) as i:
                        for j in range(2):
                            unit(2 * i + j, j, FH * P)
                    for j in range(2):
                        ends_layer = last and ffn_no == 1
                        unit(KT - 2 + j, j, 0 if ends_layer else KT * P)

            act.wait_ge(x_loaded, 16)
            act.wait_ge(vec_loaded, 96)
            act.wait_ge(const_made, 10)
            for m in range(KT):
                norm_hi(m, g1[:, m:m + 1], lambda: None)
            with act.Fori(0, DEPTH) as layer:
                for j in range(2):
                    split_hi(layer * UNITS + j, j, KT * P)
                ffn(layer, 0, 3 * layer, 0)

                U = layer * UNITS
                rms_of(3 * layer + 1)
                split_hi(U + MIX + 2, 0, KT * P)
                act.wait_ge(evacuated, U + MIX + 3)
                act.activation(agh[:, :], agf[:, :], ACT.Copy).then_inc(*act_gate.of("ag_hi"))
                with act.Fori(0, 3) as i:
                    for j in range(2):
                        split_hi(U + 2 * i + (MIX + 3 + j), (1 + j) % 2, KT * P)
                split_hi(U + ALPHA, 1, 2 * P)
                split_hi(U + ALPHA + 1, 0, KT * P)
                split_hi(U + ALPHA + 2, 1, KT * P)
                act.wait_ge(evacuated, U + ALPHA + 3)
                act.activation(tmp[:, :, :], la[:, :, :], ACT.Abs).then_inc(*act_gate.of("abs"))
                wait_for(act, act_gate, layer, "abs")
                act.activation(tmp[:, :, :], tmp[:, :, :], ACT.Exp, scale=-1.0).then_inc(*act_gate.of("exp_abs"))
                wait_for(act, act_gate, layer, "exp_abs")
                act.activation(tmp[:, :, :], tmp[:, :, :], ACT.Ln, bias=1.0).then_inc(*act_gate.of("softplus"))
                for tt, (t0, rows) in enumerate(TT):
                    wait_for(act, pe_out, layer, ("AVT", tt))
                    act.activation(av[0:rows, tt, :], bank(use_no[("AVT", tt)])[0:rows, :], ACT.Copy)\
                        .then_inc(*act_free.of(("AVT", tt)))
                wait_for(act, dve_gate, layer, "scan1")
                act.activation(eb[:, :, :], tmp[:, :, :], ACT.Exp, scale=1.0 / TAU).then_inc(*act_gate.of("exp"))
                act.activation(kinv[:, :, :], tmp[:, :, :], ACT.Exp, scale=-1.0 / TAU).then_inc(*act_gate.of("expinv"))
                split_hi(U + ALPHA + 3, 0, KT * P)
                wait_for(act, dve_gate, layer, "end1")
                act.activation(la[:, :, :], la[:, :, :], ACT.Exp, scale=1.0 / TAU).then_inc(*act_gate.of("expend"))
                for j in range(1, 4):
                    split_hi(U + ALPHA + 3 + j, j % 2, KT * P)
                act.wait_ge(evacuated, U + ALPHA + 7)
                act.activation(arT[:, :, :], arT[:, :, :], ACT.Silu).then_inc(*act_gate.of("silu_r"))
                for tt, (t0, rows) in enumerate(TT):
                    o4 = oA[0:rows, tt, :].rearrange("p (t a d) -> p t a d", t=2, a=2)
                    for par in range(2):
                        u = ("O", tt, par)
                        wait_for(act, pe_out, layer, u)
                        act.activation(o4[:, :, par, :], bank(use_no[u])[0:rows, 0:2 * A_DV].rearrange(
                            "p (t d) -> p t d", t=2), ACT.Copy).then_inc(*act_free.of(u))
                with act.Fori(0, 6) as i:
                    for j in range(2):
                        split_hi(U + 2 * i + (ALPHA + 7 + j), j, KT * P)
                wait_for(act, pool_ready, layer, "mask_bias")
                for tt, (t0, rows) in enumerate(TT):
                    wait_for(act, pe_out, layer, ("V", tt))
                    act.activation(bv[0:rows, tt, :], bank(use_no[("V", tt)])[0:rows, :], ACT.Copy)\
                        .then_inc(*act_free.of(("V", tt)))
                for s in range(len(items) + 1):
                    if s < len(items):
                        qt, h = items[s]
                        rows = TT[qt][1]
                        nk = P * (qt + 1) if qt < NTT - 1 else CACHE + DEC
                        wait_for(act, max_done, layer, (qt, h))
                        if s >= 2:
                            wait_for(act, pe_out, layer, ("PT", s - 2))
                        act.activation(pr[0:rows, s % 2, 0:nk], sc[0:rows, s % 2, 0:nk], ACT.Exp,
                                       bias=nmax[0:rows, qt, h:h + 1],
                                       accum_out=rsum[0:rows, qt, h:h + 1]).then_inc(*exp_done.of((qt, h)))
                    if s >= 1:
                        n = s - 1
                        qt, h = items[n]
                        rows = TT[qt][1]
                        wait_for(act, pe_out, layer, ("PT", n))
                        if n >= 2:
                            wait_for(act, av_done, layer, items[n - 2])
                        src = bank(use_no[("PT", n)])
                        if qt < NTT - 1:
                            act.activation(pt[:, n % 2, 0:P * (qt + 1)], src[:, 0:P * (qt + 1)], ACT.Copy)\
                                .then_inc(*act_free.of(("PT", n)))
                        else:
                            s3 = src.rearrange("p (k t) -> p k t", t=P)
                            d3 = pt[:, n % 2, :].rearrange("p (k t) -> p k t", t=P)
                            act.activation(d3[:, 0:2, 0:DEC], s3[:, 0:2, 0:DEC], ACT.Copy)
                            act.activation(d3[0:DEC, 2, 0:DEC], s3[0:DEC, 2, 0:DEC], ACT.Copy)\
                                .then_inc(*act_free.of(("PT", n)))
                wait_for(act, summed, layer, ("B", NTT - 1))
                act.activation(rr[:, :, 0:A_HEADS], ssq[:, :, 0:A_HEADS], ACT.Sqrt, bias=eps[:, :],
                               scale=1.0 / A_DV).then_inc(*act_gate.of("rms_a"))
                act.activation(rr[:, :, A_HEADS:], ssq[:, :, A_HEADS:], ACT.Sqrt, bias=eps[:, :],
                               scale=1.0 / HD).then_inc(*act_gate.of("rms_b"))
                for tt, (t0, rows) in enumerate(TT):
                    wait_for(act, dve_free, layer, ("MA", tt))
                    m3 = mixf[:, tt % 2, 0:4 * rows].rearrange("p (j t) -> p j t", j=4)
                    act.activation(zh[:, 0:4, t0:t0 + rows], m3, ACT.Copy).then_inc(*mix_hi.of(("A", tt)))
                    wait_for(act, pe_out, layer, ("MB", tt))
                    stand_alone(act)
                    src = bank(use_no[("MB", tt)])[:, 0:4 * rows].rearrange("p (j t) -> p j t", j=4)
                    act.activation(zh[:, 4:8, t0:t0 + rows], src, ACT.Copy, scale=gatt[:, bass.ds(layer, 1)])\
                        .then_inc(*mix_hi.of(("B", tt)))
                with act.Fori(0, KT // 2) as i:
                    for j in range(2):
                        split_hi(U + 2 * i + (OUT + 2 + j), j, KT * P)
                act.wait_ge(unit_done, U + (OUT + KT + 2))
                for m in range(KT):
                    norm_hi(m, g2[:, bass.ds(layer * KT + m, 1)],
                            lambda: act.wait_ge(evacuated, U + OUT + m + 3))
                ffn(layer, FFN2, 3 * layer + 2, 1)
            rms_of(3 * DEPTH)

        @block.vector
        def _(dve):
            def split_lo(U, slot, columns):
                rows = RANK if columns == 2 * P else P
                dve.wait_ge(hi_ready, U + 1)
                dve.tensor_tensor(wl[slot][0:rows, 0:columns], raw[slot][0:rows, 0:columns],
                                  wh[slot][0:rows, 0:columns].bitcast(f32), ALU.subtract).then_inc(lo_ready, 1)

            def norm_lo(m, gain, count):
                dve.wait_ge(zh_ready, count)
                dve.scalar_tensor_tensor(out=zl[:, m, :], in0=x[:, m, :], scalar=gain,
                                         in1=zh[:, m, :].bitcast(f32), op0=ALU.mult,
                                         op1=ALU.subtract).then_inc(z_ready, 1)

            def token_factor(norm):
                dve.wait_ge(rms_ready, norm + 1)
                dve.reciprocal(S[:, :], S[:, :]).then_inc(S_ready, 1)
                dve.wait_ge(S_ready, norm + 1)
                stand_alone(dve)

            def ffn(layer, first, norm, ffn_no):
                for half in range(2):
                    base = layer * UNITS + first + half * (2 * FH + KT)
                    hid = (layer * 2 + ffn_no) * (2 * FH) + half * FH
                    if half == 0:
                        token_factor(norm)

                    def tile(m, columns):
                        dve.wait_ge(unit_done, base + 2 * m + 3)
                        dve.tensor_tensor(two(tmp[:, 0, :]), pair(0), two(S[:, :]), ALU.mult).then_inc(evacuated, 1)
                        split_lo(base + 2 * m + 2, 0, columns)
                        dve.wait_ge(unit_done, base + 2 * m + 4)
                        dve.wait_ge(hid_ready, hid + m + 1)
                        dve.tensor_tensor(two(tmp[:, 1, :]), pair(1), two(S[:, :]), ALU.mult).then_inc(evacuated, 1)
                        dve.wait_ge(evacuated, base + 2 * m + 4)
                        dve.wait_ge(silu_ready, hid + m + 1)
                        dve.tensor_tensor(tmp[:, 1, :], sil[:, :], tmp[:, 1, :], ALU.mult).then_inc(hid_made, 1)
                        split_lo(base + 2 * m + 3, 1, columns)
                        dve.wait_ge(hid_hi, hid + m + 1)
                        dve.tensor_tensor(hl[:, m, :], tmp[:, 1, :], hh[:, m, :].bitcast(f32),
                                          ALU.subtract).then_inc(hid_ready, 1)

                    with dve.Fori(0, FH - 1) as m:
                        tile(m, KT * P)
                    tile(FH - 1, FH * P)

                    down = base + 2 * FH
                    last = half == 1

                    def unit(m, slot, split):
                        dve.wait_ge(unit_done, down + m + 3)
                        dve.scalar_tensor_tensor(out=two(x[:, m, :]), in0=pair(slot), scalar=0.5,
                                                 in1=two(x[:, m, :]), op0=ALU.mult, op1=ALU.add).then_inc(evacuated, 1)
                        if split:
                            split_lo(down + m + 2, slot, split)
                        if last:
                            gains, at = (gm, layer * KT) if ffn_no == 0 else (g1, (layer + 1) * KT)
                            norm_lo(m, gains[:, bass.ds(at + m, 1)], (norm + 1) * KT + m + 1)

                    with dve.Fori(0, KT // 2 - 1) as i:
                        for j in range(2):
                            unit(2 * i + j, j, FH * P)
                    for j in range(2):
                        ends_layer = last and ffn_no == 1
                        unit(KT - 2 + j, j, 0 if ends_layer else KT * P)

            dve.sem_inc(lo_ready, 2)
            dve.sem_inc(evacuated, 2)
            dve.sem_inc(hid_ready, 1)
            dve.wait_ge(ext_loaded, 16)
            far = EXT - 2 * REL - 1
            dve.tensor_copy(ext[:, 0:far], ext[:, far:far + 1].to_broadcast([DEPTH * B_HEADS, far])).then_inc(ext_made, 1)
            dve.wait_ge(ext_stored, 16)
            dve.wait_ge(x_loaded, 16)
            dve.wait_ge(vec_loaded, 96)
            dve.wait_ge(const_made, 10)
            for m in range(KT):
                norm_lo(m, g1[:, m:m + 1], m + 1)

            def project(U, slot, dst, columns):
                dve.wait_ge(unit_done, U + 3)
                dve.tensor_tensor(two(dst), pair(slot), two(S[:, :]), ALU.mult).then_inc(evacuated, 1)
                split_lo(U + 2, slot, columns)

            def head_sums(layer, k, buf, heads, at, tt):
                rows = TT[tt][1]
                wait_for(dve, squared, layer, (k, tt))
                dve.tensor_reduce(ssq[0:rows, tt, at:at + heads],
                                  mixf[0:rows, buf, :].rearrange("p (h d) -> p h d", h=heads),
                                  AX.X, ALU.add).then_inc(*summed.of((k, tt)))

            with dve.Fori(0, DEPTH) as layer:
                for j in range(2):
                    split_lo(layer * UNITS + j, j, KT * P)
                ffn(layer, 0, 3 * layer, 0)

                U = layer * UNITS
                token_factor(3 * layer + 1)
                dve.wait_ge(unit_done, U + (MIX + 3))
                dve.tensor_tensor(two(agf[:, :]), pu[0][0:RANK, :, 0:HALF], two(S[0:RANK, :]), ALU.mult)\
                    .then_inc(evacuated, 1)
                split_lo(U + (MIX + 2), 0, KT * P)
                wait_for(dve, act_gate, layer, "ag_hi")
                dve.tensor_tensor(agl[:, :], agf[:, :], agh[:, :].bitcast(f32), ALU.subtract)\
                    .then_inc(*dve_gate.of("ag_lo"))
                with dve.Fori(0, 2) as i:
                    for j in range(2):
                        project(U + 2 * i + (MIX + 1 + j), (1 + j) % 2, aqkT[:, 2 * i + j, :], KT * P)
                for j in range(4):
                    project(U + (MIX + 5 + j), (1 + j) % 2, vT[:, j, :], 2 * P if j == 2 else KT * P)
                dve.wait_ge(unit_done, U + (ALPHA + 3))
                dve.tensor_scalar(two(la[:, 1, :]), px[0][:, :, 0:HALF], balpha[:, bass.ds(2 * layer + 1, 1)], None,
                                  ALU.add).then_inc(*dve_gate.of("x1"))
                dve.tensor_scalar(two(la[:, 0, :]), pair(1), balpha[:, bass.ds(2 * layer, 1)], None,
                                  ALU.add).then_inc(evacuated, 1)
                split_lo(U + (ALPHA + 2), 1, KT * P)
                dve.wait_ge(evacuated, U + (ALPHA + 3))
                dve.tensor_scalar(kinv[:, :, :], la[:, :, :], 0.0, None, ALU.min).then_inc(*dve_gate.of("min"))
                wait_for(dve, dve_gate, layer, "min")
                wait_for(dve, act_gate, layer, "softplus")
                dve.tensor_tensor(la[:, :, :], kinv[:, :, :], tmp[:, :, :], ALU.subtract).then_inc(*dve_gate.of("logsig"))
                wait_for(dve, dve_gate, layer, "logsig")
                for t in range(2):
                    dve.tensor_tensor_scan(tmp[:, t, :], restart[:, :], la[:, t, :], 0.0, ALU.mult, ALU.add)\
                        .then_inc(*dve_gate.of(f"scan{t}"))
                project(U + (ALPHA + 1), 0, arT[:, 0, :], KT * P)
                wait_for(dve, dve_gate, layer, "scan1")
                dve.tensor_tensor(la[:, :, SEQ:T], tmp[:, :, T - 1:T].to_broadcast([P, 2, DEC]), tmp[:, :, SEQ:T],
                                  ALU.subtract).then_inc(*dve_gate.of("end_s"))
                for t in range(2):
                    sums = tmp[:, t, 0:SEQ].rearrange("p (c j) -> p c j", j=CH)
                    dve.tensor_tensor(la[:, t, 0:SEQ].rearrange("p (c j) -> p c j", j=CH),
                                      sums[:, :, CH - 1:CH].to_broadcast([P, SEQ // CH, CH]), sums,
                                      ALU.subtract).then_inc(*dve_gate.of(f"end{t}"))
                project(U + (ALPHA + 2), 1, arT[:, 1, :], KT * P)
                wait_for(dve, act_gate, layer, "exp")
                dve.scalar_tensor_tensor(out=aqkT[:, 0:2, :], in0=aqkT[:, 0:2, :], scalar=A_DK ** -0.5,
                                         in1=eb[:, :, :], op0=ALU.mult, op1=ALU.mult).then_inc(*dve_gate.of("q"))
                wait_for(dve, act_gate, layer, "expinv")
                dve.tensor_tensor(kinv[:, :, :], aqkT[:, 2:4, :], kinv[:, :, :], ALU.mult).then_inc(*dve_gate.of("kinv"))
                wait_for(dve, act_gate, layer, "expend")
                dve.tensor_tensor(aqkT[:, 2:4, :], aqkT[:, 2:4, :], la[:, :, :], ALU.mult).then_inc(*dve_gate.of("kend"))
                for j in range(2, 4):
                    project(U + (ALPHA + 1 + j), j % 2, arT[:, j, :], KT * P)

                for tt, (t0, rows) in enumerate(TT):
                    wait_for(dve, pe_out, layer, ("KT", tt))
                    dve.tensor_copy(kend[0:rows, tt, :], bank(use_no[("KT", tt)])[0:rows, 0:256])\
                        .then_inc(*dve_free.of(("KT", tt)))
                wait_for(dve, pool_ready, layer, "scores")
                for tt, (t0, rows) in enumerate(TT):
                    for par in range(2):
                        u = ("AT", tt, par)
                        wait_for(dve, pe_out, layer, u)
                        if tt >= 2:
                            wait_for(dve, pe_out, layer, ("O", tt - 2, par))
                        stand_alone(dve)
                        src = bank(use_no[u])[0:rows, 0:2 * P].rearrange("p (t i) -> p t i", t=2)
                        dve.copy_predicated(atm[0:rows, tt % 2, par, :, 0:rows], causal[0:rows, :, 0:rows].bitcast(i32),
                                            src[:, :, 0:rows]).then_inc(*dve_free.of(u))
                    sample = tt == NTT - 1
                    for c in range(1 if sample else 2):
                        n = 2 * tt + c
                        end = T - 1 if sample else n * CH + CH - 1
                        wait_for(dve, pe_out, layer, ("U", tt, c))
                        if not sample and n > 0:
                            wait_for(dve, state_made, layer, (tt, 0, 1) if c else (tt - 1, 1, 1))
                        for t in range(2):
                            old = st_s[:, t, 0, :] if sample else st[:, t, n, :]
                            new = st_s[:, t, 1, :] if sample else st[:, t, n + 1, :]
                            dve.scalar_tensor_tensor(out=new, in0=old, scalar=eb[:, t, end:end + 1],
                                                     in1=bank(use_no[("U", tt, c)])[:, t * P:t * P + A_DV],
                                                     op0=ALU.mult, op1=ALU.add).then_inc(*state_made.of((tt, c, t)))

                for dst, at in ((bqT, 0), (bkT, CACHE), (vT, 0)):
                    first = ALPHA + 5 + 4 * (dst is bkT) + 8 * (dst is vT)
                    with dve.Fori(0, 2) as i:
                        for j in range(2):
                            project(U + 2 * i + (first + j), j, dst[:, 2 * i + j, at:at + T], KT * P)
                for tt in range(NTT):
                    head_sums(layer, "A", 0, A_HEADS, 0, tt)

                wait_for(dve, pool_ready, layer, "mask_bias")

                def tile_out(qt):
                    rows = TT[qt][1]
                    wait_for(dve, exp_done, layer, (qt, B_HEADS - 1))
                    dve.reciprocal(rinv[0:rows, qt, :], rsum[0:rows, qt, :]).then_inc(*rinv_made.of(qt))
                    wait_for(dve, rinv_made, layer, qt)
                    wait_for(dve, av_done, layer, (qt, B_HEADS - 1))
                    o = pu[(qt % 4) // 2][0:rows, qt % 2, :].rearrange("p (h d) -> p h d", h=B_HEADS)
                    dve.tensor_tensor(oB[0:rows, qt, :].rearrange("p (h d) -> p h d", h=B_HEADS), o,
                                      rinv[0:rows, qt, :].unsqueeze(2).to_broadcast([rows, B_HEADS, HD]),
                                      ALU.mult).then_inc(*ob_ready.of(qt))
                    if qt >= 1:
                        head_sums(layer, "B", 1, B_HEADS, A_HEADS, qt - 1)

                for s, (qt, h) in enumerate(items):
                    rows = TT[qt][1]
                    nk, at = (P * (qt + 1), BAND - P * (qt + 1)) if qt < NTT - 1 else (CACHE + DEC, P)
                    wait_for(dve, pe_out, layer, ("SC", s))
                    if s >= 2:
                        wait_for(dve, exp_done, layer, items[s - 2])
                    row = sc[0:rows, s % 2, 0:nk]
                    dve.scalar_tensor_tensor(out=row, in0=bank(use_no[("SC", s)])[0:rows, 0:nk], scalar=HD ** -0.5,
                                             in1=bt[0:rows, h, at:at + nk], op0=ALU.mult,
                                             op1=ALU.add).then_inc(*dve_free.of(("SC", s)))
                    wait_for(dve, dve_free, layer, ("SC", s))
                    dve.tensor_reduce(nmax[0:rows, qt, h:h + 1], row, AX.X, ALU.max, negate=True)\
                        .then_inc(*max_done.of((qt, h)))
                    if qt >= 1 and h == 3:
                        tile_out(qt - 1)
                tile_out(NTT - 1)
                head_sums(layer, "B", 1, B_HEADS, A_HEADS, NTT - 1)

                wait_for(dve, act_gate, layer, "rms_b")
                dve.reciprocal(rr[:, :, :], rr[:, :, :]).then_inc(*summed.of("rr"))
                wait_for(dve, summed, layer, "rr")
                for tt, (t0, rows) in enumerate(TT):
                    for k, o, heads, at in (("A", oA, A_HEADS, 0), ("B", oB, B_HEADS, A_HEADS)):
                        o3 = o[0:rows, tt, :].rearrange("p (h d) -> p h d", h=heads)
                        f = rr[0:rows, tt, at:at + heads].unsqueeze(2).to_broadcast([rows, heads, 512 // heads])
                        dve.tensor_tensor(o3, o3, f, ALU.mult).then_inc(*normed.of((tt, k)))
                wait_for(dve, act_gate, layer, "silu_r")
                for tt, (t0, rows) in enumerate(TT):
                    def four(row):
                        return row.rearrange("p (j t) -> p j t", j=4)

                    wait_for(dve, pe_out, layer, ("MA", tt))
                    m = four(mixf[:, tt % 2, 0:4 * rows])
                    dve.scalar_tensor_tensor(out=m, in0=four(bank(use_no[("MA", tt)])[:, 0:4 * rows]),
                                             scalar=ggla[:, bass.ds(layer, 1)], in1=arT[:, :, t0:t0 + rows],
                                             op0=ALU.mult, op1=ALU.mult).then_inc(*dve_free.of(("MA", tt)))
                    wait_for(dve, mix_hi, layer, ("A", tt))
                    wait_for(dve, dve_free, layer, ("MA", tt))
                    dve.tensor_tensor(zl[:, 0:4, t0:t0 + rows], m, zh[:, 0:4, t0:t0 + rows].bitcast(f32),
                                      ALU.subtract).then_inc(*mix_ready.of(("A", tt)))
                    wait_for(dve, mix_hi, layer, ("B", tt))
                    dve.scalar_tensor_tensor(out=zl[:, 4:8, t0:t0 + rows],
                                             in0=four(bank(use_no[("MB", tt)])[:, 0:4 * rows]),
                                             scalar=gatt[:, bass.ds(layer, 1)],
                                             in1=zh[:, 4:8, t0:t0 + rows].bitcast(f32), op0=ALU.mult,
                                             op1=ALU.subtract).then_inc(*mix_ready.of(("B", tt)))

                with dve.Fori(0, KT // 2) as i:
                    for j in range(2):
                        m = 2 * i + j
                        dve.wait_ge(unit_done, U + m + (OUT + 3))
                        dve.tensor_tensor(two(x[:, m, :]), pair(j), two(x[:, m, :]), ALU.add).then_inc(evacuated, 1)
                        split_lo(U + m + (OUT + 2), j, KT * P)
                for m in range(KT):
                    norm_lo(m, g2[:, bass.ds(layer * KT + m, 1)], (3 * layer + 2) * KT + (m + 1))
                ffn(layer, FFN2, 3 * layer + 2, 1)

            token_factor(3 * DEPTH)
            for m in range(KT):
                dve.scalar_tensor_tensor(out=x[:, m, :], in0=x[:, m, :], scalar=g1[:, DEPTH * KT + m:DEPTH * KT + m + 1],
                                         in1=S[:, :], op0=ALU.mult, op1=ALU.mult).then_inc(y_ready, 1)


_OUTS = {"yT": (D_MODEL, T), "gla_prompt": (DEPTH, 2, P, A_DV), "gla_sample": (DEPTH, 2, P, A_DV),
         "new_kT": (DEPTH, 512, T), "new_v": (DEPTH, T, 512)}


def kernel(x_prompt, x_sample, state_gla, cache_k, cache_v,
           norm_ffn1, w_ffn1_gate, w_ffn1_up, w_ffn1_down,
           norm_mix, w_in, w_alpha, b_alpha, gla_norm, attn_bias, attn_norm, w_out,
           norm_ffn2, w_ffn2_gate, w_ffn2_up, w_ffn2_down, final_norm):
    import numpy as np
    import concourse.bacc as bacc
    from concourse.bass_utils import run_bass_kernel_spmd

    a = np.asarray

    def column_tiles(w):
        l, k, n = w.shape
        return a(w).reshape(l, k // P, P, n // P, P).transpose(0, 3, 2, 1, 4).reshape(l, n // P, P, k)

    def per_partition(v):
        return a(v).reshape(-1, P).T

    def gate_up(g, u):
        return np.stack([column_tiles(a(g)), column_tiles(a(u))], 2).reshape(DEPTH * 2 * FT, P, KT * P)

    def down(w):
        halves = a(w).reshape(DEPTH * 2, D_FF // 2, D_MODEL)
        return column_tiles(halves).reshape(DEPTH * 2 * KT, P, FH * P)

    wi = a(w_in)
    cut = 1024
    units_in = np.concatenate([wi[:, :, cut:cut + P], wi[:, :, :cut], wi[:, :, cut + RANK:]], 2)
    ins = {
        "xT": np.concatenate([a(x_prompt)[0], a(x_sample)[0]], 0).T,
        "bias_rev": a(attn_bias).reshape(DEPTH * B_HEADS, 2 * REL + 1)[:, ::-1],
        "gains1": per_partition(np.concatenate([a(norm_ffn1), a(final_norm)[None]], 0)),
        "gain_mix": per_partition(norm_mix), "gain2": per_partition(norm_ffn2),
        "gains_gla": per_partition(gla_norm),
        "gains_att": np.concatenate([a(attn_norm), a(attn_norm)], 1).T,
        "b_alpha": per_partition(b_alpha),
        "gate_up1": gate_up(w_ffn1_gate, w_ffn1_up), "down1": down(w_ffn1_down),
        "gate_up2": gate_up(w_ffn2_gate, w_ffn2_up), "down2": down(w_ffn2_down),
        "w_in": column_tiles(units_in).reshape(-1, P, KT * P), "w_alpha": a(w_alpha),
        "w_out": column_tiles(a(w_out)).reshape(-1, P, KT * P),
        "state": a(state_gla).reshape(DEPTH, 2, P, A_DV),
        "keysT": a(cache_k).reshape(DEPTH, CACHE, 512).transpose(0, 2, 1),
        "values": a(cache_v).reshape(DEPTH, CACHE, 512),
    }
    nc = bacc.Bacc("TRN2", target_bir_lowering=False, num_devices=1)
    arrays = {f"in_{n}": np.ascontiguousarray(v) for n, v in ins.items()}
    args = {n: nc.dram_tensor(f"in_{n}", arrays[f"in_{n}"].shape, f32, kind="ExternalInput").ap() for n in ins}
    outs = {n: nc.dram_tensor(f"out_{n}", s, f32, kind="ExternalOutput").ap() for n, s in _OUTS.items()}
    encoder_step(nc, **args, **outs)
    r = run_bass_kernel_spmd(nc, [arrays], core_ids=[0]).results[0]
    r = {n: r[f"out_{n}"] for n in _OUTS}
    y, k, v = r["yT"].T, r["new_kT"].transpose(0, 2, 1), r["new_v"]

    def heads(z):
        return np.ascontiguousarray(z).reshape(DEPTH, 1, -1, B_HEADS, HD)

    return (np.ascontiguousarray(y[:SEQ])[None], np.ascontiguousarray(y[SEQ:])[None],
            r["gla_prompt"].reshape(DEPTH, 1, A_HEADS, A_DK, A_DV), heads(k[:, :SEQ]), heads(v[:, :SEQ]),
            r["gla_sample"].reshape(DEPTH, 1, A_HEADS, A_DK, A_DV), heads(k[:, SEQ:]), heads(v[:, SEQ:]))
```

```python
from contextlib import ExitStack

import concourse.bass as bass
from concourse import mybir
from concourse.alu_op_type import AluOpType as ALU

f32 = mybir.dt.float32
f32r = mybir.dt.float32r
i32 = mybir.dt.int32
ACT = mybir.ActivationFunctionType

P = 128
DEPTH = 2
D_MODEL = 1024
D_FF = 2816
SEQ, DEC = 512, 32
T = SEQ + DEC
HALF = T // 2
KT = D_MODEL // P
FT = D_FF // P
POOL_K = KT - 4
FINAL_DVE = KT - 2
FH = FT // 2
CH = 64
A_HEADS, A_DK, A_DV, RANK = 4, 64, 128, 16
B_HEADS, HD = 8, 64
CACHE = 256
NKEY = CACHE + T
REL = 128
BAND = 512
EXT = BAND + P
TAU = 16.0
EPS = 1e-6
NEG = -1e30
TT = [(tt * P, P) for tt in range(SEQ // P)] + [(SEQ, DEC)]
NTT = len(TT)

FFN_UNITS = 2 * (2 * FH + KT)
IN_UNITS = 1 + 8 + 1 + 4 + 12
MIX = FFN_UNITS
ALPHA = MIX + 9
SIDE = ALPHA + 1
SIDE_UNITS = [("v", j) for j in range(4)] + [(c, j) for j in range(4) for c in "qk"] + [("r", j) for j in range(4)]
OUT = MIX + IN_UNITS
FFN2 = OUT + KT
UNITS = FFN2 + FFN_UNITS
assert UNITS % 2 == 0

ITEMS = [(qt, 2 * j + par) for j in range(B_HEADS // 2) for qt in range(NTT) for par in range(2)]
PAIR_ITEMS = 2 * NTT


def schedule():
    at = {}

    def spread(steps, first, end):
        for n, step in enumerate(steps):
            slot = first + n * (end - first) // len(steps)
            at.setdefault((slot // KT, slot % KT), []).append(step)

    for tt in range(NTT):
        at[(0, 2 + tt)] = [("AVT", tt)]
        at[(7, 1 + tt)] = [("V", tt), ("A_SUMS", tt)]
    gla = []
    for t in range(NTT + 1):
        gla += [("KT", t), ("AT", t)] * (t < NTT) + [("O", t - 1)] * (t >= 1) + [("U", t)] * (t < NTT)
    spread(gla, 3 * KT + 3, 7 * KT)
    spread([("ITEM", n) for n in range(len(ITEMS) + 2)], 8 * KT + 2, 16 * KT - 6)
    at[(15, 4)] = [("MERGE", 0)]
    at[(15, 5)] = [("MERGE", 1)]
    return at


SCHEDULE = schedule()
ORDER = [step for slot in sorted(SCHEDULE) for step in SCHEDULE[slot]]
MERGE = [4, 5, 6, 0, 1, 2, 3, 7]


def steps_of(unit, k=None):
    return [s for kk in (range(KT) if k is None else [k]) for s in SCHEDULE.get((unit, kk), [])]


VECTORS = {"g1": (DEPTH + 1) * KT, "gm": DEPTH * KT, "g2": DEPTH * KT,
           "ggla": DEPTH, "gatt": DEPTH, "balpha": 2 * DEPTH}


class Signal:

    def __init__(self, sem, events):
        self.sem, self.events, self.said = sem, list(events), []
        self.at = {e: i + 1 for i, e in enumerate(self.events)}
        assert len(self.at) == len(self.events)

    def value(self, layer, event):
        return layer * len(self.events) + self.at[event]

    def of(self, event):
        assert self.events[len(self.said)] == event, (event, self.events[len(self.said)])
        self.said.append(event)
        return self.sem, 1


def encoder_step(nc, xT, bias_rev, vectors,
                 gate_up1, down1, gate_up2, down2, w_in, w_alpha, w_out, state, keysT, values,
                 yT, gla_prompt, gla_sample, new_kT, new_vT):
    ctx = ExitStack()
    with ctx:
        def sb(name, shape, dt=f32, scope=ctx):
            return scope.enter_context(nc.sbuf_tensor(name, shape, dt))

        def sem(name):
            return ctx.enter_context(nc.semaphore(name))

        x = sb("x", [P, KT, T])
        zh = sb("zh", [P, KT, T], f32r)
        zl = sb("zl", [P, KT, T], f32r)
        raw = [sb(f"raw{s}", [P, FH * P]) for s in range(2)]
        wh = [sb(f"wh{s}", [P, FH * P], f32r) for s in range(2)]
        wl = [sb(f"wl{s}", [P, FH * P], f32r) for s in range(2)]
        S = sb("S", [P, T])
        sq_acc = sb("sq_acc", [P, T])
        sq_tmp = sb("sq_tmp", [P, T])
        tmp = sb("tmp", [P, 2, T])
        sil = sb("sil", [P, T])
        ones = sb("ones", [P, P])
        ident = sb("ident", [P, P])
        vec = sb("vec", [P, sum(VECTORS.values())])
        first = {name: sum(list(VECTORS.values())[:n]) for n, name in enumerate(VECTORS)}
        g1, gm, g2, ggla, gatt, balpha = (vec[:, first[name]:first[name] + VECTORS[name]] for name in VECTORS)
        eps = sb("eps", [P, 1])
        restart = sb("restart", [P, T])
        causal = sb("causal", [P, 2, P])
        ext = sb("ext", [DEPTH * B_HEADS, EXT])
        agf = sil[0:RANK, :]
        agh = sb("agh", [RANK, T], f32r)
        agl = sb("agl", [RANK, T], f32r)
        ssq = sb("ssq", [P, NTT, A_HEADS + B_HEADS])
        rr = sb("rr", [P, NTT, A_HEADS + B_HEADS])
        minus_half = sb("minus_half", [P, NTT, A_HEADS])

        with ExitStack() as ffn_scope:
            hh = sb("hh", [P, FH, T], f32r, ffn_scope)
            hl = sb("hl", [P, FH, T], f32r, ffn_scope)
        arT = sb("arT", [P, 4, T])
        oA = sb("oA", [P, NTT, 512])
        bqT = sb("bqT", [P, 4, T])
        bkT = sb("bkT", [P, 4, NKEY])
        vT = sb("vT", [P, 4, T])
        with ExitStack() as gla_scope:
            aqkT = sb("aqkT", [P, 4, T], f32, gla_scope)
            kinv = sb("kinv", [P, 2, T], f32, gla_scope)
            la = sb("la", [P, 2, T], f32, gla_scope)
            eb = sb("eb", [P, 2, T], f32, gla_scope)
            av = sb("av", [P, NTT, 512], f32, gla_scope)
            kend = sb("kend", [P, NTT, 256], f32, gla_scope)
            st = sb("st", [P, 2, SEQ // CH + 1, A_DV], f32, gla_scope)
            st_s = sb("st_s", [P, 2, 2, A_DV], f32, gla_scope)
            atm = sb("atm", [P, 2, 2, 2, P], f32, gla_scope)
        bv = sb("bv", [P, NTT, 512])
        cv = sb("cv", [P, CACHE // P, 512])
        bt = sb("bt", [P, B_HEADS, BAND])
        sc = sb("sc", [P, 2, BAND])
        pt = sb("pt", [P, 2, BAND])
        oB = sb("oB", [P, NTT, 512])
        nmax = sb("nmax", [P, NTT, B_HEADS])
        rsum = sb("rsum", [P, NTT, B_HEADS])
        rinv = sb("rinv", [P, NTT, B_HEADS])
        squares_out = tmp[:, :, :].rearrange("p a t -> p (a t)")

        pu = [ctx.enter_context(nc.psum_tensor(f"pu{s}", [P, 2, 512], f32)) for s in range(2)]
        px = [ctx.enter_context(nc.psum_tensor(f"px{s}", [P, 2, 512], f32)) for s in range(2)]
        skew = nc.dram_tensor("skew", [DEPTH, B_HEADS, P, BAND], f32, kind="Internal").ap()
        ext_dram = nc.dram_tensor("ext_dram", [DEPTH * B_HEADS, EXT], f32, kind="Internal").ap()

        def bank(n):
            return px[(n % 4) // 2][:, n % 2, :]

        def pair(s):
            return pu[s][:, :, 0:HALF]

        def across(banks):
            return banks[:, :, :].rearrange("p a b -> p (a b)")[:, 0:T]

        def two(row):
            return row.rearrange("p (a b) -> p a b", a=2)

        x_loaded = [sem(f"x_loaded{k}") for k in range(KT)]
        sq_made = sem("sq_made")
        sq_part = sem("sq_part")
        waited = sem("waited")
        vec_loaded = sem("vec_loaded")
        ext_loaded = sem("ext_loaded")
        ext_stored = sem("ext_stored")
        skew_stored = sem("skew_stored")
        const_made = sem("const_made")
        ext_made = sem("ext_made")
        raw_loaded = [sem(f"raw_loaded{s}") for s in range(2)]
        hi_ready = sem("hi_ready")
        lo_ready = sem("lo_ready")
        unit_done = sem("unit_done")
        evacuated = sem("evacuated")
        zh_ready = sem("zh_ready")
        z_ready = sem("z_ready")
        sq_step = sem("sq_step")
        stats_done = sem("stats_done")
        rms_ready = sem("rms_ready")
        S_ready = sem("S_ready")
        silu_ready = sem("silu_ready")
        hid_made = sem("hid_made")
        hid_hi = sem("hid_hi")
        hid_ready = sem("hid_ready")
        mix_loaded = sem("mix_loaded")
        gla_in = sem("gla_in")
        bias_loaded = [sem(f"bias_loaded{j}") for j in range(B_HEADS // 2)]
        cv_loaded = sem("cv_loaded")
        outs = sem("outs")
        gained = sem("gained")
        y_stored = sem("y_stored")
        y_ready = sem("y_ready")
        y_ready_pool = sem("y_ready_pool")
        OUTS = 4 * 16

        uses = []
        for kind, n in ORDER:
            if kind == "AT" or kind == "O":
                uses += [(kind, n, 0), (kind, n, 1)]
            elif kind == "U":
                uses += [("U", n, c) for c in range(2 if n < NTT - 1 else 1)]
            elif kind in ("MERGE", "A_SUMS"):
                pass
            elif kind == "ITEM":
                uses += [("SC", n)] * (n < len(ITEMS)) + [("PV", n - 2)] * (n >= 2)
                uses += [("PT", n - 1)] * (1 <= n <= len(ITEMS))
            else:
                uses.append((kind, n))
        use_no = {u: n for n, u in enumerate(uses)}

        pe_out = Signal(sem("pe_out"), uses)
        act_free = Signal(sem("act_free"), [u for u in uses if u[0] in ("AVT", "O", "V", "PT", "PV")])
        dve_free = Signal(sem("dve_free"), [u for u in uses if u[0] in ("KT", "AT", "SC")])
        state_made = Signal(sem("state_made"), [(tt, c, t) for tt in range(NTT)
                                                for c in range(2 if tt < NTT - 1 else 1) for t in range(2)])
        z_free = Signal(sem("z_free"), [("side", k) for k in MERGE[:-1]] + [("out", k) for k in range(KT - 1)])
        merged = Signal(sem("merged"), MERGE)
        gated = Signal(sem("gated"), MERGE[3:7])
        mix_hi = Signal(sem("mix_hi"), MERGE)
        mix_ready = Signal(sem("mix_ready"), MERGE)
        exp_done = Signal(sem("exp_done"), ITEMS)
        rinv_made = Signal(sem("rinv_made"), ITEMS)
        act_gate = Signal(sem("act_gate"), ["ag_hi", "abs", "exp_abs", "softplus", "exp", "expinv", "expend",
                                            "silu_r", "silu_r3"])
        dve_gate = Signal(sem("dve_gate"), ["ag_lo", "x1", "min", "logsig", "scan0", "scan1", "end_s", "end0",
                                            "end1", "q", "kinv", "kend"])
        groups = [("A", tt) for tt in range(NTT)] + [("B", j) for j in range(4)]
        head_sums = [("A", tt, h) for tt in range(NTT) for h in range(A_HEADS)] + [("B",) + item for item in ITEMS]
        summed = Signal(sem("summed"), head_sums)
        norms = ["A"] + [("B", j) for j in range(4)]
        rr_made = Signal(sem("rr_made"), [(step, g) for g in norms for step in ("mean", "rr")])
        normed = Signal(sem("normed"), groups)
        pool_ready = Signal(sem("pool_ready"), ["states", "scores", "zero_oB"] + [("bias", j) for j in range(4)])

        def wait_for(engine, signal, layer, event):
            engine.wait_ge(signal.sem, signal.value(layer, event))

        def stand_alone(engine):
            engine.sem_inc(waited, 1)

        def wait_left(engine, layer, u):
            kind = u[0]
            if kind == "U":
                wait_for(engine, state_made, layer, (u[1], u[2], 1))
            elif u in act_free.at:
                wait_for(engine, act_free, layer, u)
            else:
                wait_for(engine, dve_free, layer, u)

        block = ctx.enter_context(nc.Block())

        @block.sync
        def _(sp):
            x_rows = xT.rearrange("(k p) t -> p k t", p=P)
            sp.dma_start(ext[:, EXT - 2 * REL - 1:EXT], bias_rev).then_inc(ext_loaded, 16)
            sp.dma_start(x[:, 0, :], x_rows[:, 0, :]).then_inc(x_loaded[0], 16)
            sp.dma_start(vec[:, :], vectors).then_inc(vec_loaded, 16)
            sp.dma_start(raw[0][:, 0:KT * P], gate_up1[0]).then_inc(raw_loaded[0], 16)
            for k in range(1, KT):
                sp.dma_start(x[:, k, :], x_rows[:, k, :]).then_inc(x_loaded[k], 16)
            sp.dma_start(raw[1][:, 0:KT * P], gate_up1[1]).then_inc(raw_loaded[1], 16)

            def load(U, slot, columns, src):
                sp.wait_ge(lo_ready, U + 1)
                rows = RANK if columns == 2 * P else P
                sp.dma_start(raw[slot][0:rows, 0:columns], src).then_inc(raw_loaded[slot], 16)

            def ffn_loads(layer, first, gate_up, down):
                for half in range(2):
                    base = layer * UNITS + first + half * (2 * FH + KT)
                    with sp.Fori(1 if first == 0 and half == 0 else 0, FH) as m:
                        for j in range(2):
                            src = sp.snap(layer * (2 * FT) + 2 * m + (half * 2 * FH + j))
                            U = sp.snap(base + 2 * m + j)
                            load(U, j, KT * P, gate_up[src])
                    with sp.Fori(0, KT // 2) as i:
                        for j in range(2):
                            src = sp.snap(layer * (2 * KT) + 2 * i + (half * KT + j))
                            U = sp.snap(base + 2 * i + (2 * FH + j))
                            load(U, j, FH * P, down[src])

            with sp.Fori(0, DEPTH) as layer:
                ffn_loads(layer, 0, gate_up1, down1)
                row = layer * (IN_UNITS - 1)
                load(sp.snap(layer * UNITS + MIX), 0, KT * P, w_in[sp.snap(row)])
                with sp.Fori(0, 4) as i:
                    for j in range(2):
                        src = sp.snap(row + 2 * i + (1 + j))
                        load(sp.snap(layer * UNITS + 2 * i + (MIX + 1 + j)), (1 + j) % 2, KT * P, w_in[src])
                load(sp.snap(layer * UNITS + ALPHA), 1, 2 * P, w_alpha[layer])
                with sp.Fori(0, 8) as i:
                    for j in range(2):
                        src = sp.snap(row + 2 * i + (9 + j))
                        load(sp.snap(layer * UNITS + 2 * i + (ALPHA + 1 + j)), j, KT * P, w_in[src])
                with sp.Fori(0, KT // 2) as i:
                    for j in range(2):
                        src = sp.snap(layer * KT + 2 * i + j)
                        load(sp.snap(layer * UNITS + 2 * i + (OUT + j)), j, KT * P, w_out[src])
                ffn_loads(layer, FFN2, gate_up2, down2)
                for j in range(2):
                    load(sp.snap(layer * UNITS + (UNITS + j)), j, KT * P, gate_up1[sp.snap(layer * (2 * FT) + (2 * FT + j))])
            for m in range(KT):
                sp.wait_ge(*((y_ready, m + 1) if m < FINAL_DVE else (y_ready_pool, m + 1 - FINAL_DVE)))
                sp.dma_start(yT[m * P:(m + 1) * P, :], x[:, m, :]).then_inc(y_stored, 16)
            sp.wait_ge(y_stored, 16 * KT)
            sp.wait_ge(outs, OUTS * DEPTH)

        @block.gpsimd
        def _(pool):
            pool.memset(ones[:, :], 1.0).then_inc(const_made, 1)
            pool.memset(ident[:, :], 0.0).then_inc(const_made, 1)
            pool.memset(eps[:, :], EPS).then_inc(const_made, 1)
            pool.memset(restart[:, :], 1.0).then_inc(const_made, 1)
            pool.memset(causal[:, :, :], 1.0).then_inc(const_made, 1)
            pool.memset(ssq[:, :, :], 1.0).then_inc(const_made, 1)
            pool.memset(minus_half[:, :, :], -0.5).then_inc(const_made, 1)
            pool.wait_ge(const_made, 7)
            pool.affine_select(out=ident[:, :], in_=ident[:, :], compare_op=ALU.not_equal, fill=1.0,
                               base=0, pattern=[[-1, P]], channel_multiplier=1).then_inc(const_made, 1)
            pool.memset(restart[:, 0:T:CH], 0.0).then_inc(const_made, 1)
            pool.affine_select(out=causal[:, :, :], in_=causal[:, :, :], compare_op=ALU.is_ge, fill=0.0,
                               base=0, pattern=[[0, 2], [1, P]], channel_multiplier=-1).then_inc(const_made, 1)
            pool.wait_ge(const_made, 10)
            pool.memset(causal[0:CH, :, CH:P], 0.0).then_inc(const_made, 1)

            def squares(norm, tile_waits):
                base = norm * (2 * KT - 1)
                tile_waits(0)
                pool.tensor_tensor(sq_acc[:, :], x[:, 0, :], x[:, 0, :], ALU.mult).then_inc(sq_step, 1)
                with pool.Fori(1, KT) as m:
                    tile_waits(m)
                    pool.wait_ge(sq_step, base + 2 * m - 1)
                    pool.tensor_tensor(sq_tmp[:, :], x[:, m, :], x[:, m, :], ALU.mult).then_inc(sq_step, 1)
                    pool.wait_ge(sq_step, base + 2 * m)
                    pool.tensor_tensor(sq_acc[:, :], sq_acc[:, :], sq_tmp[:, :], ALU.add).then_inc(sq_step, 1)

            pool.wait_ge(x_loaded[0], 16)
            pool.tensor_tensor(sq_acc[:, :], x[:, 0, :], x[:, 0, :], ALU.mult).then_inc(sq_step, 1)
            for k in range(1, POOL_K):
                pool.wait_ge(x_loaded[k], 16)
                pool.wait_ge(sq_step, 2 * k - 1)
                pool.tensor_tensor(sq_tmp[:, :], x[:, k, :], x[:, k, :], ALU.mult).then_inc(sq_step, 1)
                pool.wait_ge(sq_step, 2 * k)
                pool.tensor_tensor(sq_acc[:, :], sq_acc[:, :], sq_tmp[:, :], ALU.add).then_inc(sq_step, 1)
            pool.wait_ge(sq_step, 2 * POOL_K - 1)
            pool.wait_ge(sq_part, KT - POOL_K - 1)
            pool.tensor_tensor(sq_acc[:, :], sq_acc[:, :], tmp[:, 0, :], ALU.add)\
                .then_inc(sq_step, 2 * (KT - POOL_K))
            pool.wait_ge(ext_made, 2)
            pool.dma_start(ext_dram, ext[:, :]).then_inc(ext_stored, 16)
            pool.wait_ge(ext_stored, 16)
            for n in range(0, DEPTH * B_HEADS, 2):
                l, h = n // B_HEADS, n % B_HEADS
                src = bass.AP(ext_dram.tensor, n * EXT + P - 1, [[EXT, 2], [-1, P], [1, BAND]])
                pool.dma_start(skew[l, h:h + 2], src).then_inc(skew_stored, 16)
            with pool.Fori(0, DEPTH) as layer:
                U = layer * UNITS
                squares(3 * layer + 1, lambda m: pool.wait_ge(evacuated, U + m + (FFN_UNITS - KT + 3)))
                stand_alone(pool)
                pool.dma_start(bkT[:, :, 0:CACHE], keysT[layer].rearrange("(j p) t -> p j t", p=P)).then_inc(mix_loaded, 16)
                pool.dma_start(st_s[:, :, 0, :], state[layer].rearrange("t p v -> p t v")).then_inc(gla_in, 16)
                pool.memset(st[:, :, 0, :], 0.0).then_inc(*pool_ready.of("states"))
                pool.memset(atm[:, :, :, :, :], 0.0).then_inc(*pool_ready.of("scores"))
                wait_for(pool, act_free, layer, ("O", NTT - 1, 1))
                wait_for(pool, state_made, layer, (NTT - 1, 0, 1))
                stand_alone(pool)
                pool.dma_start(gla_prompt[layer].rearrange("t p v -> p t v"), st[:, :, SEQ // CH, :]).then_inc(outs, 16)
                pool.dma_start(gla_sample[layer].rearrange("t p v -> p t v"), st_s[:, :, 1, :]).then_inc(outs, 16)
                pool.wait_ge(outs, OUTS * layer + 32)
                pool.wait_ge(skew_stored, 8 * DEPTH * B_HEADS)
                stand_alone(pool)
                for j in range(4):
                    pool.dma_start(bt[:, 2 * j:2 * j + 2, :], skew[layer, 2 * j:2 * j + 2].rearrange("h p c -> p h c"))\
                        .then_inc(bias_loaded[j], 16)
                    if j == 0:
                        pool.dma_start(cv[:, :, :], values[layer].rearrange("(c p) d -> p c d", p=P)).then_inc(cv_loaded, 16)
                pool.memset(oB[:, NTT - 1, :], 0.0).then_inc(*pool_ready.of("zero_oB"))
                for j in range(4):
                    pool.wait_ge(bias_loaded[j], 16 * layer + 16)
                    stand_alone(pool)
                    pool.memset(bt[0:CH, 2 * j:2 * j + 2, BAND - CH:BAND], NEG * HD ** 0.5)\
                        .then_inc(*pool_ready.of(("bias", j)))
                pool.wait_ge(evacuated, U + (SIDE + 6))
                stand_alone(pool)
                pool.dma_start(new_vT[layer].rearrange("(j p) t -> p j t", p=P), vT[:, :, :]).then_inc(outs, 16)

                def inverse_rms(g, heads, d):
                    n = heads.stop - heads.start
                    pool.tensor_scalar(rr[:, :, heads], ssq[:, :, heads], 1.0 / d, EPS, ALU.mult, ALU.add)\
                        .then_inc(*rr_made.of(("mean", g)))
                    wait_for(pool, rr_made, layer, ("mean", g))
                    pool.tensor_tensor(rr[:, :, heads], rr[:, :, heads], minus_half[:, :, 0:n], ALU.pow)\
                        .then_inc(*rr_made.of(("rr", g)))

                wait_for(pool, summed, layer, ("A", NTT - 1, A_HEADS - 1))
                stand_alone(pool)
                inverse_rms("A", slice(0, A_HEADS), A_DV)
                for j in range(4):
                    if j == 2:
                        pool.wait_ge(evacuated, U + (SIDE + 14))
                        stand_alone(pool)
                        pool.dma_start(new_kT[layer].rearrange("(j p) t -> p j t", p=P), bkT[:, :, CACHE:NKEY])\
                            .then_inc(outs, 16)
                    wait_for(pool, summed, layer, ("B",) + ITEMS[PAIR_ITEMS * (j + 1) - 1])
                    stand_alone(pool)
                    inverse_rms(("B", j), slice(A_HEADS + 2 * j, A_HEADS + 2 * j + 2), HD)
                pool.wait_ge(outs, OUTS * layer + OUTS)
                squares(3 * layer + 2, lambda m: pool.wait_ge(evacuated, U + m + (OUT + 3)))
                squares(3 * layer + 3, lambda m: pool.wait_ge(evacuated, U + m + (UNITS - KT + 3)))
            for m in range(FINAL_DVE, KT):
                pool.wait_ge(z_ready, 3 * DEPTH * KT + m + 1)
                pool.tensor_scalar(x[:, m, :], x[:, m, :], g1[:, DEPTH * KT + m:DEPTH * KT + m + 1], None, ALU.mult)\
                    .then_inc(gained, 1)
            for m in range(FINAL_DVE, KT):
                pool.wait_ge(gained, m + 1 - FINAL_DVE)
                pool.wait_ge(S_ready, 3 * DEPTH + 1)
                pool.tensor_tensor(x[:, m, :], x[:, m, :], S[:, :], ALU.mult).then_inc(y_ready_pool, 1)

        @block.tensor
        def _(pe):
            pe.sem_inc(unit_done, 2)

            def k_products(slot, k, hi, lo, first, last):
                for n, (w, z) in enumerate(((wh, hi), (wh, lo), (wl, hi))):
                    for a in range(2):
                        mm = pe.matmul(pu[slot][:, a, 0:HALF], w[slot][:, k * P:(k + 1) * P],
                                       z[:, k, a * HALF:(a + 1) * HALF],
                                       start=(first and n == 0), stop=(last and n == 2))
                return mm

            def products(U, slot, k_tiles, hi, lo, before_k=None, order=None, freed=None):
                pe.wait_ge(lo_ready, U + 3)
                pe.wait_ge(evacuated, U + 1)
                for n, k in enumerate(order or range(k_tiles)):
                    if before_k is not None:
                        before_k(n)
                    mm = k_products(slot, k, hi, lo, n == 0, n == k_tiles - 1)
                    if freed and n < k_tiles - 1:
                        mm.then_inc(*z_free.of((freed, k)))
                mm.then_inc(unit_done, 1)

            def stats(norm):
                pe.wait_ge(sq_step, norm * (2 * KT - 1) + (2 * KT - 1))
                for a in range(2):
                    mm = pe.matmul(px[0][:, a, 0:HALF], ones[:, :], sq_acc[:, a * HALF:(a + 1) * HALF],
                                   start=True, stop=True)
                mm.then_inc(stats_done, 1)

            def first_unit(U, norm):
                def before_k(k):
                    pe.wait_ge(z_ready, norm * KT + (k + 1))
                    if k == KT - 2:
                        stats(norm)

                products(U, 0, KT, zh, zl, before_k)

            def ffn(layer, first, norm, ffn_no):
                for half in range(2):
                    base = layer * UNITS + first + half * (2 * FH + KT)
                    if half == 0:
                        first_unit(base, norm)
                        products(base + 1, 1, KT, zh, zl)
                        start = 1
                    else:
                        start = 0
                    with pe.Fori(start, FH) as m:
                        for j in range(2):
                            products(base + 2 * m + j, j, KT, zh, zl)
                    hid = (layer * 2 + ffn_no) * (2 * FH) + half * FH
                    products(base + 2 * FH, 0, FH, hh, hl, lambda k: pe.wait_ge(hid_ready, hid + (k + 2)))
                    products(base + 2 * FH + 1, 1, FH, hh, hl)
                    with pe.Fori(1, KT // 2) as i:
                        for j in range(2):
                            products(base + 2 * i + (2 * FH + j), j, FH, hh, hl)

            def use(layer, u):
                n = use_no[u]
                if n >= 4:
                    wait_left(pe, layer, uses[n - 4])
                    stand_alone(pe)
                return bank(n)

            def transposes(layer, u, blocks, rows_in, rows_out):
                out = use(layer, u)
                for n, b in enumerate(blocks):
                    mm = pe.transpose(out[0:rows_out, n * rows_in:(n + 1) * rows_in], b, ident[0:rows_in, 0:rows_in])
                mm.then_inc(*pe_out.of(u))

            pe.wait_ge(const_made, 11)
            with pe.Fori(0, DEPTH) as layer:
                ffn(layer, 0, 3 * layer, 0)

                norm = 3 * layer + 1
                first_unit(layer * UNITS + MIX, norm)
                with pe.Fori(0, 4) as i:
                    for j in range(2):
                        products(layer * UNITS + 2 * i + (MIX + 1 + j), (1 + j) % 2, KT, zh, zl)
                pe.wait_ge(lo_ready, layer * UNITS + (ALPHA + 3))
                pe.wait_ge(evacuated, layer * UNITS + (ALPHA + 1))
                wait_for(pe, dve_gate, layer, "ag_lo")
                for t, dst in ((0, pu[1]), (1, px[0])):
                    for a in range(2):
                        for n, (w, z) in enumerate(((wh, agh), (wh, agl), (wl, agh))):
                            mm = pe.matmul(dst[:, a, 0:HALF], w[1][0:RANK, t * P:(t + 1) * P],
                                           z[:, a * HALF:(a + 1) * HALF], start=(n == 0), stop=(n == 2))
                mm.then_inc(unit_done, 1)

                def gla_added(tt):
                    wait_for(pe, act_free, layer, ("AVT", tt))
                    wait_for(pe, dve_free, layer, ("KT", tt))
                    stand_alone(pe)
                    for c in range(2 if tt < NTT - 1 else 1):
                        j = slice(c * CH, c * CH + (CH if tt < NTT - 1 else DEC))
                        out = use(layer, ("U", tt, c))
                        for h in range(A_HEADS):
                            d = slice(A_DK * (h % 2), A_DK * (h % 2) + A_DK)
                            col = (h // 2) * P
                            mm = pe.matmul(out[d, col:col + A_DV], kend[j, tt, h * A_DK:(h + 1) * A_DK],
                                           av[j, tt, h * A_DV:(h + 1) * A_DV], start=True, stop=True)
                        mm.then_inc(*pe_out.of(("U", tt, c)))

                def gla_scores(tt):
                    t0, rows = TT[tt]
                    for par in range(2):
                        d = slice(A_DK * par, A_DK * par + A_DK)
                        out = use(layer, ("AT", tt, par))
                        for t in range(2):
                            mm = pe.matmul(out[0:rows, t * P:t * P + rows], kinv[d, t, t0:t0 + rows],
                                           aqkT[d, t, t0:t0 + rows], start=True, stop=True)
                        mm.then_inc(*pe_out.of(("AT", tt, par)))

                def gla_out(tt):
                    t0, rows = TT[tt]
                    if tt == 0:
                        wait_for(pe, pool_ready, layer, "states")
                        pe.wait_ge(gla_in, 16 * layer + 16)
                    if tt < NTT - 1:
                        wait_for(pe, state_made, layer, (tt, 0, 1))
                        stand_alone(pe)
                    for par in range(2):
                        d = slice(A_DK * par, A_DK * par + A_DK)
                        out = use(layer, ("O", tt, par))
                        wait_for(pe, dve_free, layer, ("AT", tt, par))
                        stand_alone(pe)
                        for t in range(2):
                            h = 2 * t + par
                            cols = slice(t * A_DV, (t + 1) * A_DV)
                            pe.matmul(out[0:rows, cols], atm[0:rows, tt % 2, par, t, 0:rows],
                                      av[0:rows, tt, h * A_DV:(h + 1) * A_DV],
                                      start=True, stop=False, skip_group_check=True)
                            for c in range(2 if tt < NTT - 1 else 1):
                                i = slice(c * CH, c * CH + (CH if tt < NTT - 1 else DEC))
                                before = st[d, t, 2 * tt + c, :] if tt < NTT - 1 else st_s[d, t, 0, :]
                                mm = pe.matmul(out[i, cols], aqkT[d, t, t0 + i.start:t0 + i.stop], before,
                                               start=False, stop=True, skip_group_check=True)
                        mm.then_inc(*pe_out.of(("O", tt, par)))

                def item_scores(n):
                    qt, h = ITEMS[n]
                    t0, rows = TT[qt]
                    d = slice(HD * (h % 2), HD * (h % 2) + HD)
                    if n % PAIR_ITEMS == 0:
                        pe.wait_ge(evacuated, layer * UNITS + (SIDE + SIDE_UNITS.index(("k", h // 2)) + 3))
                        pe.wait_ge(mix_loaded, 16 * layer + 16)
                    out = use(layer, ("SC", n))
                    if qt < NTT - 1:
                        spans = [(0, CACHE, P * (qt + 1))]
                    else:
                        spans = [(0, 0, CACHE), (CACHE, CACHE + SEQ, DEC)]
                    for at, key, cols in spans:
                        mm = pe.matmul(out[0:rows, at:at + cols], bqT[d, h // 2, t0:t0 + rows],
                                       bkT[d, h // 2, key:key + cols], start=True, stop=True)
                    mm.then_inc(*pe_out.of(("SC", n)))

                def item_transposes(n):
                    qt, h = ITEMS[n]
                    rows = TT[qt][1]
                    out = use(layer, ("PT", n))
                    wait_for(pe, exp_done, layer, (qt, h))
                    stand_alone(pe)
                    tiles = [(kt * P, P) for kt in range(qt + 1)] if qt < NTT - 1 else [(0, P), (P, P), (2 * P, DEC)]
                    for kt, (c0, nk) in enumerate(tiles):
                        mm = pe.transpose(out[0:nk, kt * P:kt * P + rows], sc[0:rows, n % 2, c0:c0 + nk],
                                          ident[0:rows, 0:rows])
                    mm.then_inc(*pe_out.of(("PT", n)))

                def item_values(n):
                    qt, h = ITEMS[n]
                    rows = TT[qt][1]
                    if n == 0:
                        wait_for(pe, act_free, layer, ("V", NTT - 1))
                        pe.wait_ge(cv_loaded, 16 * layer + 16)
                        stand_alone(pe)
                    out = use(layer, ("PV", n))
                    wait_for(pe, act_free, layer, ("PT", n))
                    stand_alone(pe)
                    if qt < NTT - 1:
                        vs = [(P, bv[0:P, kt, h * HD:(h + 1) * HD]) for kt in range(qt + 1)]
                    else:
                        vs = [(P, cv[0:P, kt, h * HD:(h + 1) * HD]) for kt in range(2)]
                        vs += [(DEC, bv[0:DEC, NTT - 1, h * HD:(h + 1) * HD])]
                    for kt, (nk, v) in enumerate(vs):
                        mm = pe.matmul(out[0:rows, 0:HD], pt[0:nk, n % 2, kt * P:kt * P + rows], v,
                                       start=(kt == 0), stop=(kt == len(vs) - 1))
                    mm.then_inc(*pe_out.of(("PV", n)))

                def merge(n):
                    k = MERGE[n]
                    o, j = (oA, k) if k < 4 else (oB, k - 4)
                    if n == 0:
                        for u in uses[-4:]:
                            wait_left(pe, layer, u)
                    wait_for(pe, normed, layer, ("A", NTT - 1) if k < 4 else ("B", j))
                    stand_alone(pe)
                    for tt, (t0, rows) in enumerate(TT):
                        mm = pe.transpose(px[n % 2][:, t0 // BAND, t0 % BAND:t0 % BAND + rows],
                                          o[0:rows, tt, j * P:(j + 1) * P], ident[0:rows, 0:rows])
                    mm.then_inc(*merged.of(k))

                def step(kind, n):
                    if kind == "MERGE":
                        merge(n)
                    elif kind == "A_SUMS":
                        pass
                    elif kind == "AVT" or kind == "V":
                        if n == 0:
                            pe.wait_ge(evacuated, layer * UNITS + (ALPHA + 3 if kind == "AVT" else SIDE + 6))
                        t0, rows = TT[n]
                        transposes(layer, (kind, n), [vT[:, j, t0:t0 + rows] for j in range(4)], P, rows)
                    elif kind == "KT":
                        if n == 0:
                            wait_for(pe, dve_gate, layer, "kend")
                        t0, rows = TT[n]
                        transposes(layer, ("KT", n), [aqkT[:, 2 + t, t0:t0 + rows] for t in range(2)], P, rows)
                    elif kind == "AT":
                        gla_scores(n)
                    elif kind == "U":
                        gla_added(n)
                    elif kind == "O":
                        gla_out(n)
                    else:
                        if n < len(ITEMS):
                            item_scores(n)
                        if n >= 2:
                            item_values(n - 2)
                        if 1 <= n <= len(ITEMS):
                            item_transposes(n - 1)

                for b in range(len(SIDE_UNITS)):
                    def before_k(k):
                        for kind, n in steps_of(b, k):
                            step(kind, n)

                    last = b == len(SIDE_UNITS) - 1
                    products(layer * UNITS + (SIDE + b), b % 2, KT, zh, zl, before_k,
                             order=MERGE if last else None, freed="side" if last else None)

                def first_out(n):
                    k = MERGE[n]
                    wait_for(pe, mix_ready, layer, k)
                    stand_alone(pe)
                    return k_products(0, k, zh, zl, n == 0, n == KT - 1)

                pe.wait_ge(lo_ready, layer * UNITS + (OUT + 3))
                pe.wait_ge(evacuated, layer * UNITS + (OUT + 1))
                for n in range(len(MERGE) - 1):
                    if n + 2 < len(MERGE):
                        wait_for(pe, gated if MERGE[n] < 4 else mix_ready, layer, MERGE[n])
                        stand_alone(pe)
                        merge(n + 2)
                    first_out(n)
                first_out(len(MERGE) - 1).then_inc(unit_done, 1)

                products(layer * UNITS + OUT + 1, 1, KT, zh, zl)
                with pe.Fori(1, KT // 2 - 1) as i:
                    for j in range(2):
                        products(layer * UNITS + 2 * i + (OUT + j), j, KT, zh, zl)
                products(layer * UNITS + (OUT + KT - 2), 0, KT, zh, zl)
                products(layer * UNITS + (OUT + KT - 1), 1, KT, zh, zl, freed="out")

                ffn(layer, FFN2, 3 * layer + 2, 1)
            stats(3 * DEPTH)

        @block.scalar
        def _(act):
            def split_hi(U, slot, columns):
                rows = RANK if columns == 2 * P else P
                act.wait_ge(raw_loaded[slot], (U - slot) * 8 + 16)
                act.wait_ge(unit_done, U + 1)
                act.activation(wh[slot][0:rows, 0:columns], raw[slot][0:rows, 0:columns], ACT.Copy).then_inc(hi_ready, 1)

            def norm_hi(m, gain, wait):
                wait()
                act.activation(zh[:, m, :], x[:, m, :], ACT.Copy, scale=gain).then_inc(zh_ready, 1)

            def rms_of(norm):
                act.wait_ge(stats_done, norm + 1)
                act.activation(two(S[:, :]), px[0][:, :, 0:HALF], ACT.Sqrt, bias=eps[:, :],
                               scale=1.0 / D_MODEL).then_inc(rms_ready, 1)

            def ffn(layer, first, norm, ffn_no):
                for half in range(2):
                    base = layer * UNITS + first + half * (2 * FH + KT)
                    hid = (layer * 2 + ffn_no) * (2 * FH) + half * FH

                    def tile(m, columns):
                        split_hi(base + 2 * m + 2, 0, columns)
                        act.wait_ge(evacuated, base + 2 * m + 3)
                        act.activation(sil[:, :], tmp[:, 0, :], ACT.Silu).then_inc(silu_ready, 1)
                        split_hi(base + 2 * m + 3, 1, columns)
                        act.wait_ge(hid_made, hid + m + 1)
                        act.activation(hh[:, m, :], tmp[:, 1, :], ACT.Copy).then_inc(hid_hi, 1)

                    if half == 0:
                        rms_of(norm)
                    with act.Fori(0, FH - 1) as m:
                        tile(m, KT * P)
                    tile(FH - 1, FH * P)

                    down = base + 2 * FH
                    last = half == 1

                    def unit(m, slot, split):
                        split_hi(down + m + 2, slot, split)
                        if last:
                            gains, at = (gm, layer * KT) if ffn_no == 0 else (g1, (layer + 1) * KT)
                            norm_hi(m, gains[:, bass.ds(at + m, 1)],
                                    lambda: act.wait_ge(evacuated, down + m + 3))

                    with act.Fori(0, KT // 2 - 1) as i:
                        for j in range(2):
                            unit(2 * i + j, j, FH * P)
                    for j in range(2):
                        unit(KT - 2 + j, j, KT * P)

            act.wait_ge(vec_loaded, 16)
            for m in range(KT):
                norm_hi(m, g1[:, m:m + 1], lambda: act.wait_ge(x_loaded[m], 16))
                if m == 0:
                    split_hi(0, 0, KT * P)
            for k in range(POOL_K, KT):
                act.activation((tmp[:, 0, :], tmp[:, 1, :], sil[:, :], S[:, :])[k - POOL_K], x[:, k, :], ACT.Square)\
                    .then_inc(sq_made, 1)
            act.wait_ge(const_made, 11)
            split_hi(1, 1, KT * P)
            with act.Fori(0, DEPTH) as layer:
                ffn(layer, 0, 3 * layer, 0)

                U = layer * UNITS
                rms_of(3 * layer + 1)
                split_hi(U + MIX + 2, 0, KT * P)
                act.wait_ge(evacuated, U + MIX + 3)
                act.activation(agh[:, :], agf[:, :], ACT.Copy).then_inc(*act_gate.of("ag_hi"))
                with act.Fori(0, 3) as i:
                    for j in range(2):
                        split_hi(U + 2 * i + (MIX + 3 + j), (1 + j) % 2, KT * P)
                split_hi(U + ALPHA, 1, 2 * P)
                split_hi(U + ALPHA + 1, 0, KT * P)
                split_hi(U + ALPHA + 2, 1, KT * P)
                act.wait_ge(evacuated, U + ALPHA + 3)
                act.activation(tmp[:, :, :], la[:, :, :], ACT.Abs).then_inc(*act_gate.of("abs"))
                wait_for(act, act_gate, layer, "abs")
                act.activation(tmp[:, :, :], tmp[:, :, :], ACT.Exp, scale=-1.0).then_inc(*act_gate.of("exp_abs"))
                wait_for(act, act_gate, layer, "exp_abs")
                act.activation(tmp[:, :, :], tmp[:, :, :], ACT.Ln, bias=1.0).then_inc(*act_gate.of("softplus"))
                for tt, (t0, rows) in enumerate(TT):
                    wait_for(act, pe_out, layer, ("AVT", tt))
                    act.activation(av[0:rows, tt, :], bank(use_no[("AVT", tt)])[0:rows, :], ACT.Copy)\
                        .then_inc(*act_free.of(("AVT", tt)))
                wait_for(act, dve_gate, layer, "scan1")
                act.activation(eb[:, :, :], tmp[:, :, :], ACT.Exp, scale=1.0 / TAU).then_inc(*act_gate.of("exp"))
                act.activation(kinv[:, :, :], tmp[:, :, :], ACT.Exp, scale=-1.0 / TAU).then_inc(*act_gate.of("expinv"))
                split_hi(U + ALPHA + 3, 0, KT * P)
                wait_for(act, dve_gate, layer, "end1")
                act.activation(la[:, :, :], la[:, :, :], ACT.Exp, scale=1.0 / TAU).then_inc(*act_gate.of("expend"))
                split_hi(U + ALPHA + 4, 1, KT * P)

                def item_exp(n):
                    qt, h = ITEMS[n]
                    rows = TT[qt][1]
                    nk = P * (qt + 1) if qt < NTT - 1 else CACHE + DEC
                    wait_for(act, dve_free, layer, ("SC", n))
                    act.activation(sc[0:rows, n % 2, 0:nk], sc[0:rows, n % 2, 0:nk], ACT.Exp, scale=-1.0,
                                   bias=nmax[0:rows, qt, h:h + 1],
                                   accum_out=rsum[0:rows, qt, h:h + 1]).then_inc(*exp_done.of((qt, h)))

                def item_probs(n):
                    qt = ITEMS[n][0]
                    wait_for(act, pe_out, layer, ("PT", n))
                    if n >= 2:
                        wait_for(act, pe_out, layer, ("PV", n - 2))
                    src = bank(use_no[("PT", n)])
                    if qt < NTT - 1:
                        act.activation(pt[:, n % 2, 0:P * (qt + 1)], src[:, 0:P * (qt + 1)], ACT.Copy)\
                            .then_inc(*act_free.of(("PT", n)))
                    else:
                        s3 = src.rearrange("p (k t) -> p k t", t=P)
                        d3 = pt[:, n % 2, :].rearrange("p (k t) -> p k t", t=P)
                        act.activation(d3[:, 0:2, 0:DEC], s3[:, 0:2, 0:DEC], ACT.Copy)
                        act.activation(d3[0:DEC, 2, 0:DEC], s3[0:DEC, 2, 0:DEC], ACT.Copy)\
                            .then_inc(*act_free.of(("PT", n)))

                def item_out(n):
                    qt, h = ITEMS[n]
                    rows = TT[qt][1]
                    if n == 0:
                        wait_for(act, pool_ready, layer, "zero_oB")
                    wait_for(act, rinv_made, layer, (qt, h))
                    wait_for(act, pe_out, layer, ("PV", n))
                    stand_alone(act)
                    act.activation(oB[0:rows, qt, h * HD:(h + 1) * HD], bank(use_no[("PV", n)])[0:rows, 0:HD], ACT.Copy,
                                   scale=rinv[0:rows, qt, h:h + 1]).then_inc(*act_free.of(("PV", n)))

                def step(kind, n):
                    if kind == "O":
                        rows = TT[n][1]
                        o4 = oA[0:rows, n, :].rearrange("p (t a d) -> p t a d", t=2, a=2)
                        for par in range(2):
                            u = ("O", n, par)
                            wait_for(act, pe_out, layer, u)
                            act.activation(o4[:, :, par, :], bank(use_no[u])[0:rows, 0:2 * A_DV].rearrange(
                                "p (t d) -> p t d", t=2), ACT.Copy).then_inc(*act_free.of(u))
                    elif kind == "V":
                        rows = TT[n][1]
                        if n == 0:
                            act.wait_ge(outs, OUTS * layer + 32)
                            stand_alone(act)
                        wait_for(act, pe_out, layer, ("V", n))
                        act.activation(bv[0:rows, n, :], bank(use_no[("V", n)])[0:rows, :], ACT.Copy)\
                            .then_inc(*act_free.of(("V", n)))
                    elif kind == "ITEM":
                        if n >= 2:
                            item_out(n - 2)
                        if n < len(ITEMS):
                            item_exp(n)
                        if 1 <= n <= len(ITEMS):
                            item_probs(n - 1)

                for b in range(2, len(SIDE_UNITS)):
                    for kind, n in steps_of(b):
                        step(kind, n)
                    if b == len(SIDE_UNITS) - 1:
                        act.wait_ge(evacuated, U + (OUT + 1))
                        act.activation(arT[:, 0:3, :], arT[:, 0:3, :], ACT.Silu).then_inc(*act_gate.of("silu_r"))
                    else:
                        split_hi(U + (SIDE + 2 + b), b % 2, KT * P)
                for n, k in enumerate(MERGE):
                    if k < 4:
                        wait_for(act, gated, layer, k)
                        act.activation(zh[:, k, :], tmp[:, n % 2, :], ACT.Copy).then_inc(*mix_hi.of(k))
                    else:
                        wait_for(act, merged, layer, k)
                        stand_alone(act)
                        if n < 2:
                            wait_for(act, z_free, layer, ("side", k))
                            stand_alone(act)
                        elif n == 2:
                            act.wait_ge(unit_done, U + (OUT + 2))
                            stand_alone(act)
                        act.activation(zh[:, k, :], across(px[n % 2]), ACT.Copy, scale=gatt[:, bass.ds(layer, 1)])\
                            .then_inc(*mix_hi.of(k))
                    if n == 1:
                        split_hi(U + (OUT + 1), 1, KT * P)
                        act.wait_ge(evacuated, U + (OUT + 2))
                        act.activation(arT[:, 3, :], arT[:, 3, :], ACT.Silu).then_inc(*act_gate.of("silu_r3"))
                with act.Fori(0, KT // 2 - 1) as i:
                    for j in range(2):
                        split_hi(U + 2 * i + (OUT + 2 + j), j, KT * P)
                split_hi(U + (OUT + KT), 0, KT * P)
                for m in range(KT):
                    if m < KT - 1:
                        wait_for(act, z_free, layer, ("out", m))
                    else:
                        act.wait_ge(unit_done, U + (OUT + KT + 2))
                    stand_alone(act)
                    norm_hi(m, g2[:, bass.ds(layer * KT + m, 1)],
                            lambda: act.wait_ge(evacuated, U + OUT + m + 3))
                split_hi(U + (OUT + KT + 1), 1, KT * P)
                ffn(layer, FFN2, 3 * layer + 2, 1)
            rms_of(3 * DEPTH)

        @block.vector
        def _(dve):
            def split_lo(U, slot, columns):
                rows = RANK if columns == 2 * P else P
                dve.wait_ge(hi_ready, U + 1)
                dve.tensor_tensor(wl[slot][0:rows, 0:columns], raw[slot][0:rows, 0:columns],
                                  wh[slot][0:rows, 0:columns].bitcast(f32), ALU.subtract).then_inc(lo_ready, 1)

            def norm_lo(m, gain, count):
                dve.wait_ge(zh_ready, count)
                dve.scalar_tensor_tensor(out=zl[:, m, :], in0=x[:, m, :], scalar=gain,
                                         in1=zh[:, m, :].bitcast(f32), op0=ALU.mult,
                                         op1=ALU.subtract).then_inc(z_ready, 1)

            def token_factor(norm):
                dve.wait_ge(rms_ready, norm + 1)
                dve.reciprocal(S[:, :], S[:, :]).then_inc(S_ready, 1)
                dve.wait_ge(S_ready, norm + 1)
                stand_alone(dve)

            def ffn(layer, first, norm, ffn_no):
                for half in range(2):
                    base = layer * UNITS + first + half * (2 * FH + KT)
                    hid = (layer * 2 + ffn_no) * (2 * FH) + half * FH
                    if half == 0:
                        token_factor(norm)

                    def tile(m, columns):
                        dve.wait_ge(unit_done, base + 2 * m + 3)
                        dve.tensor_tensor(two(tmp[:, 0, :]), pair(0), two(S[:, :]), ALU.mult).then_inc(evacuated, 1)
                        split_lo(base + 2 * m + 2, 0, columns)
                        dve.wait_ge(unit_done, base + 2 * m + 4)
                        dve.wait_ge(hid_ready, hid + m + 1)
                        dve.tensor_tensor(two(tmp[:, 1, :]), pair(1), two(S[:, :]), ALU.mult).then_inc(evacuated, 1)
                        dve.wait_ge(evacuated, base + 2 * m + 4)
                        dve.wait_ge(silu_ready, hid + m + 1)
                        dve.tensor_tensor(tmp[:, 1, :], sil[:, :], tmp[:, 1, :], ALU.mult).then_inc(hid_made, 1)
                        split_lo(base + 2 * m + 3, 1, columns)
                        dve.wait_ge(hid_hi, hid + m + 1)
                        dve.tensor_tensor(hl[:, m, :], tmp[:, 1, :], hh[:, m, :].bitcast(f32),
                                          ALU.subtract).then_inc(hid_ready, 1)

                    with dve.Fori(0, FH - 1) as m:
                        tile(m, KT * P)
                    tile(FH - 1, FH * P)

                    down = base + 2 * FH
                    last = half == 1

                    def unit(m, slot, split):
                        dve.wait_ge(unit_done, down + m + 3)
                        dve.scalar_tensor_tensor(out=two(x[:, m, :]), in0=pair(slot), scalar=0.5,
                                                 in1=two(x[:, m, :]), op0=ALU.mult, op1=ALU.add).then_inc(evacuated, 1)
                        split_lo(down + m + 2, slot, split)
                        if last:
                            gains, at = (gm, layer * KT) if ffn_no == 0 else (g1, (layer + 1) * KT)
                            norm_lo(m, gains[:, bass.ds(at + m, 1)], (norm + 1) * KT + m + 1)

                    with dve.Fori(0, KT // 2 - 1) as i:
                        for j in range(2):
                            unit(2 * i + j, j, FH * P)
                    for j in range(2):
                        unit(KT - 2 + j, j, KT * P)

            dve.sem_inc(lo_ready, 2)
            dve.sem_inc(evacuated, 2)
            dve.sem_inc(hid_ready, 1)
            dve.wait_ge(ext_loaded, 16)
            far = EXT - 2 * REL - 1
            dve.tensor_scalar(ext[:, 0:far], ext[:, far:far + 1].to_broadcast([DEPTH * B_HEADS, far]), HD ** 0.5, None,
                              ALU.mult).then_inc(ext_made, 1)
            dve.wait_ge(ext_made, 1)
            dve.tensor_scalar(ext[:, far:EXT], ext[:, far:EXT], HD ** 0.5, None, ALU.mult).then_inc(ext_made, 1)
            dve.wait_ge(vec_loaded, 16)
            for m in range(KT):
                dve.wait_ge(x_loaded[m], 16)
                norm_lo(m, g1[:, m:m + 1], m + 1)
                if m == 0:
                    split_lo(0, 0, KT * P)
            for n, part in enumerate((tmp[:, 1, :], sil[:, :], S[:, :])):
                dve.wait_ge(sq_made, n + 2)
                if n:
                    dve.wait_ge(sq_part, n)
                dve.tensor_tensor(tmp[:, 0, :], tmp[:, 0, :], part, ALU.add).then_inc(sq_part, 1)
            dve.wait_ge(const_made, 11)

            def project(U, slot, dst, columns):
                dve.wait_ge(unit_done, U + 3)
                dve.tensor_tensor(two(dst), pair(slot), two(S[:, :]), ALU.mult).then_inc(evacuated, 1)
                split_lo(U + 2, slot, columns)

            split_lo(1, 1, KT * P)
            with dve.Fori(0, DEPTH) as layer:
                ffn(layer, 0, 3 * layer, 0)

                U = layer * UNITS
                token_factor(3 * layer + 1)
                dve.wait_ge(unit_done, U + (MIX + 3))
                dve.tensor_tensor(two(agf[:, :]), pu[0][0:RANK, :, 0:HALF], two(S[0:RANK, :]), ALU.mult)\
                    .then_inc(evacuated, 1)
                split_lo(U + (MIX + 2), 0, KT * P)
                wait_for(dve, act_gate, layer, "ag_hi")
                dve.tensor_tensor(agl[:, :], agf[:, :], agh[:, :].bitcast(f32), ALU.subtract)\
                    .then_inc(*dve_gate.of("ag_lo"))
                with dve.Fori(0, 2) as i:
                    for j in range(2):
                        project(U + 2 * i + (MIX + 1 + j), (1 + j) % 2, aqkT[:, 2 * i + j, :], KT * P)
                for j in range(4):
                    project(U + (MIX + 5 + j), (1 + j) % 2, vT[:, j, :], 2 * P if j == 2 else KT * P)
                dve.wait_ge(unit_done, U + (ALPHA + 3))
                dve.tensor_scalar(two(la[:, 1, :]), px[0][:, :, 0:HALF], balpha[:, bass.ds(2 * layer + 1, 1)], None,
                                  ALU.add).then_inc(*dve_gate.of("x1"))
                dve.tensor_scalar(two(la[:, 0, :]), pair(1), balpha[:, bass.ds(2 * layer, 1)], None,
                                  ALU.add).then_inc(evacuated, 1)
                split_lo(U + (ALPHA + 2), 1, KT * P)
                dve.wait_ge(evacuated, U + (ALPHA + 3))
                dve.tensor_scalar(kinv[:, :, :], la[:, :, :], 0.0, None, ALU.min).then_inc(*dve_gate.of("min"))
                wait_for(dve, dve_gate, layer, "min")
                wait_for(dve, act_gate, layer, "softplus")
                dve.tensor_tensor(la[:, :, :], kinv[:, :, :], tmp[:, :, :], ALU.subtract).then_inc(*dve_gate.of("logsig"))
                wait_for(dve, dve_gate, layer, "logsig")
                for t in range(2):
                    dve.tensor_tensor_scan(tmp[:, t, :], restart[:, :], la[:, t, :], 0.0, ALU.mult, ALU.add)\
                        .then_inc(*dve_gate.of(f"scan{t}"))
                project(U + SIDE, 0, vT[:, 0, :], KT * P)
                wait_for(dve, dve_gate, layer, "scan1")
                dve.tensor_tensor(la[:, :, SEQ:T], tmp[:, :, T - 1:T].to_broadcast([P, 2, DEC]), tmp[:, :, SEQ:T],
                                  ALU.subtract).then_inc(*dve_gate.of("end_s"))
                for t in range(2):
                    sums = tmp[:, t, 0:SEQ].rearrange("p (c j) -> p c j", j=CH)
                    dve.tensor_tensor(la[:, t, 0:SEQ].rearrange("p (c j) -> p c j", j=CH),
                                      sums[:, :, CH - 1:CH].to_broadcast([P, SEQ // CH, CH]), sums,
                                      ALU.subtract).then_inc(*dve_gate.of(f"end{t}"))
                project(U + (SIDE + 1), 1, vT[:, 1, :], KT * P)
                wait_for(dve, act_gate, layer, "exp")
                dve.scalar_tensor_tensor(out=aqkT[:, 0:2, :], in0=aqkT[:, 0:2, :], scalar=A_DK ** -0.5,
                                         in1=eb[:, :, :], op0=ALU.mult, op1=ALU.mult).then_inc(*dve_gate.of("q"))
                wait_for(dve, act_gate, layer, "expinv")
                dve.tensor_tensor(kinv[:, :, :], aqkT[:, 2:4, :], kinv[:, :, :], ALU.mult).then_inc(*dve_gate.of("kinv"))
                wait_for(dve, act_gate, layer, "expend")
                dve.tensor_tensor(aqkT[:, 2:4, :], aqkT[:, 2:4, :], la[:, :, :], ALU.mult).then_inc(*dve_gate.of("kend"))

                def gla_scores(tt):
                    rows = TT[tt][1]
                    if tt == 0:
                        wait_for(dve, pool_ready, layer, "scores")
                    for par in range(2):
                        u = ("AT", tt, par)
                        wait_for(dve, pe_out, layer, u)
                        if tt >= 2:
                            wait_for(dve, pe_out, layer, ("O", tt - 2, par))
                        stand_alone(dve)
                        src = bank(use_no[u])[0:rows, 0:2 * P].rearrange("p (t i) -> p t i", t=2)
                        dve.copy_predicated(atm[0:rows, tt % 2, par, :, 0:rows], causal[0:rows, :, 0:rows].bitcast(i32),
                                            src[:, :, 0:rows]).then_inc(*dve_free.of(u))

                def gla_state(tt):
                    sample = tt == NTT - 1
                    if tt == 0:
                        wait_for(dve, pool_ready, layer, "states")
                    if sample:
                        dve.wait_ge(gla_in, 16 * layer + 16)
                    for c in range(1 if sample else 2):
                        n = 2 * tt + c
                        end = T - 1 if sample else n * CH + CH - 1
                        wait_for(dve, pe_out, layer, ("U", tt, c))
                        if not sample and n > 0:
                            wait_for(dve, state_made, layer, (tt, 0, 1) if c else (tt - 1, 1, 1))
                        stand_alone(dve)
                        for t in range(2):
                            old = st_s[:, t, 0, :] if sample else st[:, t, n, :]
                            new = st_s[:, t, 1, :] if sample else st[:, t, n + 1, :]
                            dve.scalar_tensor_tensor(out=new, in0=old, scalar=eb[:, t, end:end + 1],
                                                     in1=bank(use_no[("U", tt, c)])[:, t * P:t * P + A_DV],
                                                     op0=ALU.mult, op1=ALU.add).then_inc(*state_made.of((tt, c, t)))

                def item_bias(n):
                    qt, h = ITEMS[n]
                    rows = TT[qt][1]
                    nk, at = (P * (qt + 1), BAND - P * (qt + 1)) if qt < NTT - 1 else (CACHE + DEC, P)
                    if n % PAIR_ITEMS == 0:
                        wait_for(dve, pool_ready, layer, ("bias", h // 2))
                    wait_for(dve, pe_out, layer, ("SC", n))
                    if n >= 2:
                        wait_for(dve, pe_out, layer, ("PT", n - 2))
                    stand_alone(dve)
                    dve.tensor_tensor_reduce(out=sc[0:rows, n % 2, 0:nk], in0=bank(use_no[("SC", n)])[0:rows, 0:nk],
                                             in1=bt[0:rows, h, at:at + nk], scale=-HD ** -0.5, scalar=3e38,
                                             op0=ALU.add, op1=ALU.min, accum_out=nmax[0:rows, qt, h:h + 1])\
                        .then_inc(*dve_free.of(("SC", n)))

                def item_inverse(n):
                    qt, h = ITEMS[n]
                    rows = TT[qt][1]
                    wait_for(dve, exp_done, layer, (qt, h))
                    dve.reciprocal(rinv[0:rows, qt, h:h + 1], rsum[0:rows, qt, h:h + 1]).then_inc(*rinv_made.of((qt, h)))

                def head_sum(key, o, out):
                    n = head_sums.index(key)
                    cols = out.shape[1]
                    if n >= 8:
                        wait_for(dve, summed, layer, head_sums[n - 8])
                        stand_alone(dve)
                    dve.tensor_tensor_reduce(out=squares_out[0:rows_of(key), (n % 8) * P:(n % 8) * P + o.shape[1]], in0=o,
                                             in1=o, scale=1.0, scalar=0.0, op0=ALU.mult, op1=ALU.add,
                                             accum_out=out).then_inc(*summed.of(key))

                def rows_of(key):
                    return TT[key[1]][1]

                def item_sum(n):
                    qt, h = ITEMS[n]
                    rows = TT[qt][1]
                    wait_for(dve, act_free, layer, ("PV", n))
                    stand_alone(dve)
                    head_sum(("B", qt, h), oB[0:rows, qt, h * HD:(h + 1) * HD],
                             ssq[0:rows, qt, A_HEADS + h:A_HEADS + h + 1])

                def a_norm(tt):
                    rows = TT[tt][1]
                    wait_for(dve, rr_made, layer, ("rr", "A"))
                    stand_alone(dve)
                    o3 = oA[0:rows, tt, :].rearrange("p (h d) -> p h d", h=A_HEADS)
                    f = rr[0:rows, tt, 0:A_HEADS].unsqueeze(2).to_broadcast([rows, A_HEADS, A_DV])
                    dve.tensor_tensor(o3, o3, f, ALU.mult).then_inc(*normed.of(("A", tt)))

                def pair_norm(j):
                    wait_for(dve, rr_made, layer, ("rr", ("B", j)))
                    o = oB[:, :, j * P:(j + 1) * P].rearrange("p n (h d) -> p n h d", h=2)
                    f = rr[:, :, A_HEADS + 2 * j:A_HEADS + 2 * j + 2].unsqueeze(3).to_broadcast([P, NTT, 2, HD])
                    dve.tensor_tensor(o, o, f, ALU.mult).then_inc(*normed.of(("B", j)))

                def step(kind, n):
                    if kind == "KT":
                        rows = TT[n][1]
                        wait_for(dve, pe_out, layer, ("KT", n))
                        dve.tensor_copy(kend[0:rows, n, :], bank(use_no[("KT", n)])[0:rows, 0:256])\
                            .then_inc(*dve_free.of(("KT", n)))
                    elif kind == "AT":
                        gla_scores(n)
                    elif kind == "U":
                        gla_state(n)
                    elif kind == "A_SUMS":
                        rows = TT[n][1]
                        wait_for(dve, act_free, layer, ("O", n, 1))
                        stand_alone(dve)
                        for h in range(A_HEADS):
                            head_sum(("A", n, h), oA[0:rows, n, h * A_DV:(h + 1) * A_DV], ssq[0:rows, n, h:h + 1])
                    elif kind == "ITEM":
                        if n < len(ITEMS):
                            item_bias(n)
                        if 1 <= n <= len(ITEMS):
                            item_inverse(n - 1)
                        if n >= 3:
                            item_sum(n - 3)
                        if 5 <= n < 5 + 2 * NTT and n % 2:
                            a_norm((n - 5) // 2)
                        if n > PAIR_ITEMS and n < len(ITEMS) and n % PAIR_ITEMS == 6:
                            pair_norm(n // PAIR_ITEMS - 1)

                where = {"v": (vT, 0), "q": (bqT, 0), "k": (bkT, CACHE), "r": (arT, 0)}
                for b, (what, j) in enumerate(SIDE_UNITS):
                    if b < 2:
                        continue
                    for kind, n in steps_of(b):
                        step(kind, n)
                    dst, at = where[what]
                    if b < len(SIDE_UNITS) - 1:
                        project(U + (SIDE + b), b % 2, dst[:, j, at:at + T], KT * P)
                def gate(n):
                    k = MERGE[n]
                    wait_for(dve, merged, layer, k)
                    wait_for(dve, act_gate, layer, "silu_r3" if k == 3 else "silu_r")
                    if n == 3:
                        wait_for(dve, summed, layer, head_sums[-1])
                    if n >= 5:
                        wait_for(dve, mix_ready, layer, MERGE[n - 2])
                    stand_alone(dve)
                    dve.scalar_tensor_tensor(out=tmp[:, n % 2, :], in0=across(px[n % 2]),
                                             scalar=ggla[:, bass.ds(layer, 1)], in1=arT[:, k, :],
                                             op0=ALU.mult, op1=ALU.mult).then_inc(*gated.of(k))

                def lo_part(n):
                    k = MERGE[n]
                    wait_for(dve, mix_hi, layer, k)
                    if k < 4:
                        wait_for(dve, gated, layer, k)
                        stand_alone(dve)
                        dve.tensor_tensor(zl[:, k, :], tmp[:, n % 2, :], zh[:, k, :].bitcast(f32),
                                          ALU.subtract).then_inc(*mix_ready.of(k))
                    else:
                        stand_alone(dve)
                        dve.scalar_tensor_tensor(out=zl[:, k, :], in0=across(px[n % 2]),
                                                 scalar=gatt[:, bass.ds(layer, 1)], in1=zh[:, k, :].bitcast(f32),
                                                 op0=ALU.mult, op1=ALU.subtract).then_inc(*mix_ready.of(k))

                item_sum(len(ITEMS) - 1)
                lo_part(0)
                lo_part(1)
                project(U + (OUT - 1), 1, arT[:, 3, :], KT * P)
                lo_part(2)
                pair_norm(3)
                gate(3)
                for n in range(3, 7):
                    if n < 6:
                        gate(n + 1)
                    lo_part(n)
                lo_part(7)

                def add_out(m, slot):
                    dve.wait_ge(unit_done, U + m + (OUT + 3))
                    dve.tensor_tensor(two(x[:, m, :]), pair(slot), two(x[:, m, :]), ALU.add).then_inc(evacuated, 1)

                with dve.Fori(0, KT // 2 - 1) as i:
                    for j in range(2):
                        add_out(2 * i + j, j)
                        split_lo(U + 2 * i + (OUT + 2 + j), j, KT * P)
                add_out(KT - 2, 0)
                split_lo(U + (OUT + KT), 0, KT * P)
                for m in range(KT - 1):
                    norm_lo(m, g2[:, bass.ds(layer * KT + m, 1)], (3 * layer + 2) * KT + (m + 1))
                add_out(KT - 1, 1)
                norm_lo(KT - 1, g2[:, bass.ds(layer * KT + (KT - 1), 1)], (3 * layer + 2) * KT + KT)
                split_lo(U + (OUT + KT + 1), 1, KT * P)
                ffn(layer, FFN2, 3 * layer + 2, 1)

            token_factor(3 * DEPTH)
            for m in range(FINAL_DVE):
                dve.scalar_tensor_tensor(out=x[:, m, :], in0=x[:, m, :], scalar=g1[:, DEPTH * KT + m:DEPTH * KT + m + 1],
                                         in1=S[:, :], op0=ALU.mult, op1=ALU.mult).then_inc(y_ready, 1)


_OUTS = {"yT": (D_MODEL, T), "gla_prompt": (DEPTH, 2, P, A_DV), "gla_sample": (DEPTH, 2, P, A_DV),
         "new_kT": (DEPTH, 512, T), "new_vT": (DEPTH, 512, T)}


def kernel(x_prompt, x_sample, state_gla, cache_k, cache_v,
           norm_ffn1, w_ffn1_gate, w_ffn1_up, w_ffn1_down,
           norm_mix, w_in, w_alpha, b_alpha, gla_norm, attn_bias, attn_norm, w_out,
           norm_ffn2, w_ffn2_gate, w_ffn2_up, w_ffn2_down, final_norm):
    import numpy as np
    import concourse.bacc as bacc
    from concourse.bass_utils import run_bass_kernel_spmd

    a = np.asarray

    def column_tiles(w):
        l, k, n = w.shape
        return a(w).reshape(l, k // P, P, n // P, P).transpose(0, 3, 2, 1, 4).reshape(l, n // P, P, k)

    def per_partition(v):
        return a(v).reshape(-1, P).T

    def gate_up(g, u):
        return np.stack([column_tiles(a(g)), column_tiles(a(u))], 2).reshape(DEPTH * 2 * FT, P, KT * P)

    def down(w):
        halves = a(w).reshape(DEPTH * 2, D_FF // 2, D_MODEL)
        return column_tiles(halves).reshape(DEPTH * 2 * KT, P, FH * P)

    wi = a(w_in)
    cut = 1024
    start = {"r": cut + RANK, "q": cut + RANK + 512, "k": cut + RANK + 1024, "v": cut + RANK + 1536}
    units_in = np.concatenate([wi[:, :, cut:cut + P], wi[:, :, :cut]]
                              + [wi[:, :, start[c] + j * P:start[c] + (j + 1) * P] for c, j in SIDE_UNITS], 2)
    gate_up1 = gate_up(w_ffn1_gate, w_ffn1_up)
    ins = {
        "xT": np.concatenate([a(x_prompt)[0], a(x_sample)[0]], 0).T,
        "bias_rev": a(attn_bias).reshape(DEPTH * B_HEADS, 2 * REL + 1)[:, ::-1],
        "vectors": np.concatenate([
            per_partition(np.concatenate([a(norm_ffn1), a(final_norm)[None]], 0)), per_partition(norm_mix),
            per_partition(norm_ffn2), per_partition(gla_norm), np.concatenate([a(attn_norm), a(attn_norm)], 1).T,
            per_partition(b_alpha)], 1),
        "gate_up1": np.concatenate([gate_up1, gate_up1[:2]], 0), "down1": down(w_ffn1_down),
        "gate_up2": gate_up(w_ffn2_gate, w_ffn2_up), "down2": down(w_ffn2_down),
        "w_in": column_tiles(units_in).reshape(-1, P, KT * P), "w_alpha": a(w_alpha),
        "w_out": column_tiles(a(w_out)).reshape(-1, P, KT * P),
        "state": a(state_gla).reshape(DEPTH, 2, P, A_DV),
        "keysT": a(cache_k).reshape(DEPTH, CACHE, 512).transpose(0, 2, 1),
        "values": a(cache_v).reshape(DEPTH, CACHE, 512),
    }
    nc = bacc.Bacc("TRN2", target_bir_lowering=False, num_devices=1)
    arrays = {f"in_{n}": np.ascontiguousarray(v) for n, v in ins.items()}
    args = {n: nc.dram_tensor(f"in_{n}", arrays[f"in_{n}"].shape, f32, kind="ExternalInput").ap() for n in ins}
    outs = {n: nc.dram_tensor(f"out_{n}", s, f32, kind="ExternalOutput").ap() for n, s in _OUTS.items()}
    encoder_step(nc, **args, **outs)
    r = run_bass_kernel_spmd(nc, [arrays], core_ids=[0]).results[0]
    r = {n: r[f"out_{n}"] for n in _OUTS}
    y, k, v = r["yT"].T, r["new_kT"].transpose(0, 2, 1), r["new_vT"].transpose(0, 2, 1)

    def heads(z):
        return np.ascontiguousarray(z).reshape(DEPTH, 1, -1, B_HEADS, HD)

    return (np.ascontiguousarray(y[:SEQ])[None], np.ascontiguousarray(y[SEQ:])[None],
            r["gla_prompt"].reshape(DEPTH, 1, A_HEADS, A_DK, A_DV), heads(k[:, :SEQ]), heads(v[:, :SEQ]),
            r["gla_sample"].reshape(DEPTH, 1, A_HEADS, A_DK, A_DV), heads(k[:, SEQ:]), heads(v[:, SEQ:]))
```
